# Optimizing a Trainium2 kernel written in Bass

```python
import math
import jax, jax.numpy as jnp
from jax import lax
import numpy as np

D_MODEL = 1024
BATCH = 1
SEQ = 256
DEPTH = 2
DEC_BATCH = 8
DEC_SEQ = 1
PAST_LEN = 1024
PAGE_SIZE = 128

N_MIXERS = 2
N_CONV_LAYERS = (DEPTH + 1) // 2
N_ATTN_LAYERS = DEPTH // 2
PLE_DIM = 256
EPS = 1e-6
D_CONV = D_MODEL
CONV_WIDTH = 31
N_HEADS = 16
QK_NOPE_DIM = 64
QK_ROPE_DIM = 32
V_HEAD_DIM = 64
Q_LORA = 384
KV_LORA = 256
ROPE_THETA = 10000.0
ATTN_SCALE = 1.0 / math.sqrt(QK_NOPE_DIM + QK_ROPE_DIM)
Q_BLOCK = 128
N_GROUPS = 4
EXPERTS_PER_GROUP = 8
N_EXPERTS = N_GROUPS * EXPERTS_PER_GROUP
TOP_K = 2
D_EXPERT = 256

kernel_name = "hybrid_conv_mla_hmoe_decode_step"

def rmsnorm(x, g):
    xf = x.astype(jnp.float32)
    y = xf * lax.rsqrt(jnp.mean(xf * xf, axis=-1, keepdims=True) + EPS)
    return (y * g.astype(jnp.float32)).astype(x.dtype)

def layernorm(x, g, b):
    xf = x.astype(jnp.float32)
    mu = jnp.mean(xf, axis=-1, keepdims=True)
    var = jnp.mean(jnp.square(xf - mu), axis=-1, keepdims=True)
    y = (xf - mu) * lax.rsqrt(var + EPS) * g.astype(jnp.float32) + b.astype(jnp.float32)
    return y.astype(x.dtype)

def rope(x, pos):
    half = QK_ROPE_DIM // 2
    inv_freq = jnp.power(jnp.float32(ROPE_THETA), -jnp.arange(half, dtype=jnp.float32) / half)
    ang = pos.astype(jnp.float32)[:, None] * inv_freq[None, :]
    ang = ang.reshape(ang.shape[:1] + (1,) * (x.ndim - 3) + (half,))
    cos, sin = jnp.cos(ang), jnp.sin(ang)
    xf = x.astype(jnp.float32)
    x1, x2 = xf[..., :half], xf[..., half:]
    return jnp.concatenate([x1 * cos - x2 * sin, x1 * sin + x2 * cos], axis=-1).astype(x.dtype)

def conformer_conv(h, buf, w_pw1, b_pw1, w_dw, b_dw, ln_g, ln_b, w_pw2):
    u = h @ w_pw1 + b_pw1
    u = u[..., :D_CONV] * jax.nn.sigmoid(u[..., D_CONV:])
    full = jnp.concatenate([buf.astype(u.dtype), u], axis=1)
    z = lax.conv_general_dilated(
        full, w_dw[:, None, :].astype(u.dtype), (1,), 'VALID',
        dimension_numbers=('NWC', 'WIO', 'NWC'), feature_group_count=D_CONV) + b_dw
    z = jax.nn.silu(layernorm(z, ln_g, ln_b))
    return z @ w_pw2, full[:, -(CONV_WIDTH - 1):]

def latent_attend(q_lat, q_pe, c_kv, k_pe, mask):
    s = (jnp.einsum('bqhl,bkl->bhqk', q_lat, c_kv)
         + jnp.einsum('bqhr,bkr->bhqk', q_pe, k_pe)).astype(jnp.float32) * ATTN_SCALE
    s = jnp.where(mask[None, None], s, -jnp.inf)
    p = jax.nn.softmax(s, axis=-1).astype(c_kv.dtype)
    return jnp.einsum('bhqk,bkl->bqhl', p, c_kv)

def mla_mixer(h, pos, past_ckv, past_kpe, w_dq, g_q, w_uq, w_dkv, g_kv, w_uk, w_uv, w_o):
    B, T, _ = h.shape
    c_q = rmsnorm(h @ w_dq, g_q)
    q = (c_q @ w_uq).reshape(B, T, N_HEADS, QK_NOPE_DIM + QK_ROPE_DIM)
    q_pe = rope(q[..., QK_NOPE_DIM:], pos)
    q_lat = jnp.einsum('bthn,lhn->bthl', q[..., :QK_NOPE_DIM], w_uk)
    kv = h @ w_dkv
    c_kv = rmsnorm(kv[..., :KV_LORA], g_kv)
    k_pe = rope(kv[..., KV_LORA:], pos)
    if past_ckv is None:
        nb = T // Q_BLOCK
        qb_lat = q_lat.reshape(B, nb, Q_BLOCK, N_HEADS, KV_LORA).swapaxes(0, 1)
        qb_pe = q_pe.reshape(B, nb, Q_BLOCK, N_HEADS, QK_ROPE_DIM).swapaxes(0, 1)
        k_idx = jnp.arange(T)

        def block(args):
            b, ql, qp = args
            q_idx = b * Q_BLOCK + jnp.arange(Q_BLOCK)
            return latent_attend(ql, qp, c_kv, k_pe, k_idx[None, :] <= q_idx[:, None])

        o_lat = lax.map(block, (jnp.arange(nb), qb_lat, qb_pe))
        o_lat = o_lat.swapaxes(0, 1).reshape(B, T, N_HEADS, KV_LORA)
    else:
        P = past_ckv.shape[1]
        keys_ckv = jnp.concatenate([past_ckv.astype(c_kv.dtype), c_kv], axis=1)
        keys_kpe = jnp.concatenate([past_kpe.astype(k_pe.dtype), k_pe], axis=1)
        mask = jnp.arange(P + T)[None, :] <= P + jnp.arange(T)[:, None]
        o_lat = latent_attend(q_lat, q_pe, keys_ckv, keys_kpe, mask)
    o = jnp.einsum('bthl,lhv->bthv', o_lat, w_uv).reshape(B, T, N_HEADS * V_HEAD_DIM)
    return o @ w_o, c_kv, k_pe

def hier_moe(h, w_group, b_group, w_expert, b_expert, w_gate, w_up, w_down):
    B, T, _ = h.shape
    hf = h.astype(jnp.float32)
    g_prob = jax.nn.softmax(hf @ w_group.astype(jnp.float32) + b_group.astype(jnp.float32), axis=-1)
    grp = jnp.argmax(g_prob, axis=-1)
    g_w = jnp.take_along_axis(g_prob, grp[..., None], axis=-1)
    e_logits = (hf @ w_expert.astype(jnp.float32) + b_expert.astype(jnp.float32)).reshape(
        B, T, N_GROUPS, EXPERTS_PER_GROUP)
    e_in = jnp.take_along_axis(e_logits, grp[..., None, None], axis=2)[:, :, 0]
    top_w, top_i = lax.top_k(jax.nn.softmax(e_in, axis=-1), TOP_K)
    top_w = top_w / jnp.sum(top_w, axis=-1, keepdims=True)
    expert_id = grp[..., None] * EXPERTS_PER_GROUP + top_i
    gates = jnp.sum(jax.nn.one_hot(expert_id, N_EXPERTS, dtype=jnp.float32)
                    * (g_w * top_w)[..., None], axis=-2).astype(h.dtype)
    a = jnp.einsum('btd,edf->btef', h, w_gate)
    u = jnp.einsum('btd,edf->btef', h, w_up)
    return jnp.einsum('btef,efd->btd', jax.nn.silu(a) * u * gates[..., None], w_down)

def setup_inputs(seed: int = 0) -> dict:
    key = jax.random.key(seed)
    ks = jax.random.split(key, 36)
    f32 = jnp.float32

    def nrm(k, shape, scale):
        return scale * jax.random.normal(k, shape, f32)

    def gain(k, shape):
        return 1.0 + 0.05 * jax.random.normal(k, shape, f32)

    n_pages = PAST_LEN // PAGE_SIZE
    n_used = DEC_BATCH * n_pages
    n_pool = n_used + n_used // 4
    page_table = jax.random.permutation(ks[7], n_pool)[:n_used].reshape(DEC_BATCH, n_pages).astype(jnp.int32)
    R = QK_ROPE_DIM
    return {
        "x_prompt": nrm(ks[0], (BATCH, SEQ, D_MODEL), 1.0),
        "x_sample": nrm(ks[1], (DEC_BATCH, DEC_SEQ, D_MODEL), 1.0),
        "p_prompt": nrm(ks[2], (DEPTH, BATCH, SEQ, PLE_DIM), 1.0),
        "p_sample": nrm(ks[3], (DEPTH, DEC_BATCH, DEC_SEQ, PLE_DIM), 1.0),
        "state_conv": nrm(ks[4], (N_CONV_LAYERS, DEC_BATCH, CONV_WIDTH - 1, D_CONV), 0.5),
        "cache_ckv": nrm(ks[5], (n_pool, N_ATTN_LAYERS, PAGE_SIZE, KV_LORA), 1.0),
        "cache_kpe": nrm(ks[6], (n_pool, N_ATTN_LAYERS, PAGE_SIZE, R), 1.0),
        "page_table": page_table,
        "norm_mix": gain(ks[8], (DEPTH, D_MODEL)),
        "norm_ffn": gain(ks[9], (DEPTH, D_MODEL)),
        "norm_final": gain(ks[10], (D_MODEL,)),
        "conv_w_pw1": nrm(ks[11], (N_CONV_LAYERS, D_MODEL, 2 * D_CONV), D_MODEL ** -0.5),
        "conv_b_pw1": nrm(ks[12], (N_CONV_LAYERS, 2 * D_CONV), 0.02),
        "conv_w_dw": nrm(ks[13], (N_CONV_LAYERS, CONV_WIDTH, D_CONV), CONV_WIDTH ** -0.5),
        "conv_b_dw": nrm(ks[14], (N_CONV_LAYERS, D_CONV), 0.02),
        "conv_ln_g": gain(ks[15], (N_CONV_LAYERS, D_CONV)),
        "conv_ln_b": nrm(ks[16], (N_CONV_LAYERS, D_CONV), 0.02),
        "conv_w_pw2": nrm(ks[17], (N_CONV_LAYERS, D_CONV, D_MODEL), D_CONV ** -0.5),
        "mla_w_dq": nrm(ks[18], (N_ATTN_LAYERS, D_MODEL, Q_LORA), D_MODEL ** -0.5),
        "mla_g_q": gain(ks[19], (N_ATTN_LAYERS, Q_LORA)),
        "mla_w_uq": nrm(ks[20], (N_ATTN_LAYERS, Q_LORA, N_HEADS * (QK_NOPE_DIM + R)), Q_LORA ** -0.5),
        "mla_w_dkv": nrm(ks[21], (N_ATTN_LAYERS, D_MODEL, KV_LORA + R), D_MODEL ** -0.5),
        "mla_g_kv": gain(ks[22], (N_ATTN_LAYERS, KV_LORA)),
        "mla_w_uk": nrm(ks[23], (N_ATTN_LAYERS, KV_LORA, N_HEADS, QK_NOPE_DIM), KV_LORA ** -0.5),
        "mla_w_uv": nrm(ks[24], (N_ATTN_LAYERS, KV_LORA, N_HEADS, V_HEAD_DIM), KV_LORA ** -0.5),
        "mla_w_o": nrm(ks[25], (N_ATTN_LAYERS, N_HEADS * V_HEAD_DIM, D_MODEL), (N_HEADS * V_HEAD_DIM) ** -0.5),
        "moe_w_group": nrm(ks[26], (DEPTH, D_MODEL, N_GROUPS), D_MODEL ** -0.5),
        "moe_b_group": nrm(ks[27], (DEPTH, N_GROUPS), 0.01),
        "moe_w_expert": nrm(ks[28], (DEPTH, D_MODEL, N_EXPERTS), D_MODEL ** -0.5),
        "moe_b_expert": nrm(ks[29], (DEPTH, N_EXPERTS), 0.01),
        "moe_w_gate": nrm(ks[30], (DEPTH, N_EXPERTS, D_MODEL, D_EXPERT), D_MODEL ** -0.5),
        "moe_w_up": nrm(ks[31], (DEPTH, N_EXPERTS, D_MODEL, D_EXPERT), D_MODEL ** -0.5),
        "moe_w_down": nrm(ks[32], (DEPTH, N_EXPERTS, D_EXPERT, D_MODEL), D_EXPERT ** -0.5),
        "ple_w_in": nrm(ks[33], (DEPTH, PLE_DIM, D_MODEL), PLE_DIM ** -0.5),
        "ple_g": gain(ks[34], (DEPTH, D_MODEL)),
        "ple_w_gate": nrm(ks[35], (DEPTH, D_MODEL, D_MODEL), D_MODEL ** -0.5),
    }

def reference(x_prompt, x_sample, p_prompt, p_sample, state_conv, cache_ckv, cache_kpe, page_table,
              norm_mix, norm_ffn, norm_final,
              conv_w_pw1, conv_b_pw1, conv_w_dw, conv_b_dw, conv_ln_g, conv_ln_b, conv_w_pw2,
              mla_w_dq, mla_g_q, mla_w_uq, mla_w_dkv, mla_g_kv, mla_w_uk, mla_w_uv, mla_w_o,
              moe_w_group, moe_b_group, moe_w_expert, moe_b_expert, moe_w_gate, moe_w_up, moe_w_down,
              ple_w_in, ple_g, ple_w_gate):

    def run(x, p, pos, conv_bufs, past_fn):
        h = x
        new_conv, new_ckv, new_kpe = [], [], []
        for i in range(DEPTH):
            j = i // N_MIXERS
            hn = rmsnorm(h, norm_mix[i])
            if i % N_MIXERS == 0:
                mix, buf = conformer_conv(hn, conv_bufs[j], conv_w_pw1[j], conv_b_pw1[j], conv_w_dw[j],
                                          conv_b_dw[j], conv_ln_g[j], conv_ln_b[j], conv_w_pw2[j])
                new_conv.append(buf)
            else:
                past_ckv, past_kpe = past_fn(j)
                mix, c_kv, k_pe = mla_mixer(hn, pos, past_ckv, past_kpe, mla_w_dq[j], mla_g_q[j], mla_w_uq[j],
                                            mla_w_dkv[j], mla_g_kv[j], mla_w_uk[j], mla_w_uv[j], mla_w_o[j])
                new_ckv.append(c_kv)
                new_kpe.append(k_pe)
            h = h + mix
            h = h + hier_moe(rmsnorm(h, norm_ffn[i]), moe_w_group[i], moe_b_group[i], moe_w_expert[i],
                             moe_b_expert[i], moe_w_gate[i], moe_w_up[i], moe_w_down[i])
            h = h + (p[i] @ ple_w_in[i]) * jax.nn.sigmoid(rmsnorm(h, ple_g[i]) @ ple_w_gate[i])
        return rmsnorm(h, norm_final), jnp.stack(new_conv), jnp.stack(new_ckv), jnp.stack(new_kpe)

    pos_prompt = jnp.arange(x_prompt.shape[1], dtype=jnp.int32)
    zero_bufs = jnp.zeros((N_CONV_LAYERS, x_prompt.shape[0], CONV_WIDTH - 1, D_CONV), x_prompt.dtype)
    y_prompt, conv_state_prompt, ckv_prompt, kpe_prompt = run(
        x_prompt, p_prompt, pos_prompt, zero_bufs, lambda j: (None, None))

    n_seq = page_table.shape[0]
    pos_sample = PAST_LEN + jnp.arange(x_sample.shape[1], dtype=jnp.int32)

    def gather_past(j):
        ckv = cache_ckv[page_table, j].reshape(n_seq, -1, KV_LORA)
        kpe = cache_kpe[page_table, j].reshape(n_seq, -1, QK_ROPE_DIM)
        return ckv, kpe

    y_sample, conv_state_sample, ckv_sample, kpe_sample = run(
        x_sample, p_sample, pos_sample, state_conv, gather_past)

    return (y_prompt, y_sample, conv_state_prompt, conv_state_sample,
            ckv_prompt, kpe_prompt, ckv_sample, kpe_sample)


_drawn_inputs = setup_inputs


def setup_inputs(seed=0):
    import zlib

    import numpy as np

    out = dict(_drawn_inputs(seed))
    spreads = {}
    factors = {}
    for name, (base, spread) in spreads.items():
        noise = np.random.default_rng([zlib.crc32(name.encode()), seed]).standard_normal(out[name].shape)
        drawn = base * np.exp(spread * noise) if base else spread * noise
        out[name] = __import__('jax').numpy.asarray(drawn.astype(out[name].dtype))
    for name, factor in factors.items():
        out[name] = (out[name] * factor).astype(out[name].dtype)
    return out
```

```python
from contextlib import ExitStack

import numpy as np

import concourse.bass as bass
from concourse import mybir

F32 = mybir.dt.float32
I32 = mybir.dt.int32
U32 = mybir.dt.uint32
ALU = mybir.AluOpType
ACT = mybir.ActivationFunctionType
AX = mybir.AxisListType

P = 128
D = 1024
KD = D // P
TP, TS = 256, 8
T = TP + TS
TILES = [(0, 128), (128, 128), (256, TS)]
EPS = 1e-6
CW = 31
E, G, EG = 32, 4, 8
F = 256
FK = F // P
NPAIR = 2 * T
W = 64
XCOLS = NPAIR + W
NXW = (T + W - 1) // W - 1
HALF = NPAIR // 2
NST = (NPAIR + P - 1) // P
PLE = 256
H, DN, DR, DV = 16, 64, 32, 64
QL, KL = 384, 256
KQ, KK = QL // P, KL // P
PAGES, PAGE = 8, 128
PAST = PAGES * PAGE
SCALE = float(1.0 / np.sqrt(DN + DR))
NEG = -1e30
BIG = 3e38
SLOT = 2048
NSLOT = 9
ARENA = 21760

C_ID, C_ONE, C_TRI, C_ROT, C_COS, C_SIN = 0, 128, 256, 384, 512, 512 + T
C_MASK = C_SIN + T
C_IOTA = C_MASK + 384
C_GRP = C_IOTA + NPAIR
C_W64 = C_GRP + E
C_ALL = C_W64 + NXW * E

VEC = [("norm_mix", 2 * KD), ("norm_ffn", 2 * KD), ("ple_g", 2 * KD), ("norm_final", KD), ("conv_ln_g", KD),
       ("conv_ln_b", KD), ("conv_b_dw", KD), ("conv_b_pw1", 2 * KD), ("mla_g_q", KQ), ("mla_g_kv", KK)]
VCOL, NVEC = {}, 0
for _name, _n in VEC:
    VCOL[_name] = NVEC
    NVEC += _n

G_PW1, G_PW2, G_MOE0 = 0, 8, 12
G_PLE0 = G_MOE0 + 3 * E
G_DQ = G_PLE0 + 5
G_DKV, G_UQ, G_UK, G_UV, G_WO = G_DQ + 2, G_DQ + 4, G_DQ + 7, G_DQ + 8, G_DQ + 9
G_MOE1 = G_WO + 4
G_PLE1 = G_MOE1 + 3 * E
NPIECE = G_PLE1 + 5
G_MOE, G_PLE = [G_MOE0, G_MOE1], [G_PLE0, G_PLE1]

NORMS = []
SQ = {}
_n = 0
for _name, _c in [("n0", 8), ("ln", 8), ("n1", 8), ("n2", 8), ("n3", 8), ("q", KQ), ("kv", KK), ("n4", 8), ("n5", 8),
                  ("n6", 8)]:
    NORMS.append(_name if _name != 'ln' else 'lnv')
    SQ[_name] = _n
    _n += _c


def constants():
    c = np.zeros((P, C_ALL), np.float32)
    i = np.arange(P)
    c[:, C_ID:C_ID + P] = np.eye(P)
    c[:, C_ONE:C_ONE + P] = 1
    c[:, C_TRI:C_TRI + P] = i[:, None] < i[None, :]
    for m in range(P):
        if m % DR < DR // 2:
            c[m + DR // 2, C_ROT + m] = -1
        else:
            c[m - DR // 2, C_ROT + m] = 1
    pos = np.concatenate([np.arange(TP), np.full(TS, PAST)]).astype(np.float32)
    freq = np.power(np.float32(10000.0), -np.arange(DR // 2, dtype=np.float32) / np.float32(DR // 2))
    ang = (pos[None, :] * freq[i % (DR // 2)][:, None]).astype(np.float32)
    c[:, C_COS:C_COS + T] = np.cos(ang)
    c[:, C_SIN:C_SIN + T] = np.sin(ang)
    later = np.where(i[None, :] > i[:, None], NEG, 0)
    c[:, C_MASK:C_MASK + P] = later
    c[:, C_MASK + 2 * P:C_MASK + 3 * P] = later
    c[:, C_IOTA:C_IOTA + NPAIR] = np.arange(NPAIR)
    c[:, C_GRP:C_GRP + E] = np.arange(E) // EG
    c[:, C_W64:] = np.repeat(W * np.arange(1, NXW + 1), E)
    return c


def build(nc, a, out):
    with ExitStack() as ctx:
        def sb(name, shape, dt=F32):
            return ctx.enter_context(nc.sbuf_tensor(name, shape, dt))

        def sem(name):
            return ctx.enter_context(nc.semaphore(name))

        ring = sb("ring", [P, NSLOT, SLOT])
        cst = sb("cst", [P, C_ALL])
        hT = sb("hT", [P, KD, T])
        xnT = sb("xnT", [P, KD, T])
        sq = sb("sq", [P, KD, T])
        pT = sb("pT", [P, 2, 2, T])
        vt = sb("vt", [P, NVEC])
        wdw = sb("wdw", [P, CW * KD])
        wr = sb("wr", [P, 2, KD, G + E])
        br = sb("br", [P, 2, G + E])
        rstd = sb("rstd", [P, T])
        pages = sb("pages", [1, TS * PAGES], I32)
        arena = sb("arena", [P, ARENA])
        bank = [ctx.enter_context(nc.psum_tensor(f"bank{i}", [P, 512], F32)) for i in range(8)]

        def place(at, *shape):
            n = int(np.prod(shape))
            v = arena[:, at:at + n]
            if len(shape) == 2:
                v = v.rearrange("p (a b) -> p a b", a=shape[0])
            elif len(shape) == 3:
                v = v.rearrange("p (a b c) -> p a b c", a=shape[0], b=shape[1])
            return v, at + n

        uT, q = place(0, KD, CW - 1 + TP)
        zT, q = place(q, KD, T)
        stT, q = place(q, KD, TS, CW)
        sgu, q = place(q, 2, T)
        ctmp, q = place(q, TS, CW)
        mu, q = place(q, T)
        XR, q = place(0, 3, D)
        S, q = place(q, 3, NPAIR)
        exw, _ = place(0, 3, SLOT)
        OutR, _ = place(0, NST, D)
        XGT, q = place(3 * SLOT, KD, XCOLS)
        OutT, q = place(q, KD, XCOLS)
        SG, q = place(q, 3, NPAIR)
        Gm, q = place(q, NST, T)
        q_xe = q
        xe, q = place(q, 3, KD, W)
        hid, q = place(q, 3, FK, W)
        sg, q = place(q, 3, FK, W)
        rt = {}
        for name, n in (("L", G + E), ("gl8", 8), ("gmx", 8), ("em", E), ("G32", E), ("emx", 8), ("M1", E), ("M2", E),
                        ("M", E), ("pos", E), ("ex", 5), ("eidx", 2), ("gidx", 1), ("gsum", 1), ("den", 1), ("w1", 1),
                        ("w2", 1), ("slot1", 1), ("slot2", 1)):
            rt[name] = sb("rt_" + name, [P, 3, n])
        gix = sb("gix", [P, 3, 8], U32)
        eix = sb("eix", [P, 3, 8], U32)
        cnt = sb("cnt", [P, E])
        incl = sb("incl", [P, E])
        off = sb("off", [P, E])
        most = sb("most", [P, 1])
        offI = sb("offI", [P, E], I32)
        mostI = sb("mostI", [P, 1], I32)
        xst = sb("xst", [P, NXW, E])
        xfl = sb("xfl", [P, NXW, E])
        xstI = sb("xstI", [P, NXW, E], I32)
        tiny = sb("tiny", [P, 2])
        sgp, q = place(q_xe, 2, T)
        tgp, q = place(q, 2, T)
        qnT, q = place(0, KD, T)
        qpeT, q = place(q, 4, T)
        oT, q = place(q, KD, T)
        wukT = oT.rearrange("p a b -> p (a b)")[:, 0:KD * KL].rearrange("p (a b) -> p a b", a=KD)
        ckvT, q = place(q, KK, T)
        kpeT, q = place(q, T)
        ckR, q = place(q, KL)
        qlat, q = place(q, KK, TS, H)
        olat, q = place(q, KK, H, TS)
        qps, q = place(q, TS, H)
        b0 = q
        knT, q = place(b0, KD, TP)
        V, q = place(q, 2, H * DV)
        b1 = q
        sS, q = place(q, 2, 384)
        pr, q = place(q, 2, 384)
        PT, q = place(q, 4, 384)
        b2 = q
        CN, q2 = place(b0, TS, KL)
        sc, q2 = place(q2, PAST + 1)
        pp, q2 = place(q2, PAST + 1)
        assert q2 <= q
        CK, q = place(q, 2, PAGES * KL)
        KPT, q = place(q, 2, PAST)
        PTs, q = place(q, PAGES + 1, H)
        qpr, q = place(q, 4, T)
        cqr, q2 = place(b1, KQ, T)
        kvr, q2 = place(q2, KK, T)
        kr, q2 = place(q2, T)
        rtmp, q2 = place(q2, 2, T)
        cqT, q2 = place(q2, KQ, T)
        assert q2 <= b2
        stat, q = place(q, 8 * H)
        sstat = stat[:, 6 * H:8 * H]
        assert q <= ARENA, q
        CKT = [x[:].rearrange("p a b -> p (a b)")[:, 0:KK * PAST].rearrange("p (g k t) -> p g k t", g=PAGES, k=KK)
               for x in (xnT, sq)]

        ident = cst[:, C_ID:C_ID + P]
        ones = cst[:, C_ONE:C_ONE + P]
        tri = cst[:, C_TRI:C_TRI + P]

        full = [sem(f"bank_full{i}") for i in range(8)]
        free = [sem(f"bank_free{i}") for i in range(8)]
        w_in = [sem(f"w_in{i}") for i in range(NSLOT)]
        s_cst, s_x, s_vec, s_dw, s_st, s_p, s_wr, s_pg = (sem("in_" + n) for n in
                                                         ("cst", "x", "vec", "dw", "st", "p", "wr", "pages"))
        s_uk = sem("in_ukT")
        s_sq = sem("squares")
        s_xn = sem("xn_chunks")
        s_rs = sem("roots")
        s_dve = sem("dve_steps")
        s_act = sem("act_steps")
        s_pl = sem("pool_steps")
        s_cv = sem("conv_steps")
        s_z = sem("conv_chunks")
        s_zc = sem("centred_chunks")
        s_zn = sem("normed_chunks")
        s_zs = sem("silu_chunks")
        s_zero = sem("pads_zeroed")
        s_pad = sem("window_pad_zeroed")
        s_ex = sem("router_exp")
        s_pre = sem("router_diffs")
        s_hot = sem("pair_masks")
        s_w = sem("pair_gates")
        s_slot = sem("pair_slots")
        s_S = sem("selection")
        s_SG = sem("gated_selection")
        s_off = sem("offsets")
        s_xe = sem("window_in")
        s_gu = sem("gate_up_done")
        s_sg = sem("silu_done")
        s_hid = sem("hidden_done")
        s_dn = sem("down_done")
        s_out = sem("window_out")
        s_mo = sem("moe_out")
        s_ple = sem("h_embedded")
        x_w, x_xe, x_gu, x_sg, x_hid, x_dn, x_out = ([sem(f"x{i}_{n}") for i in range(2)] for n in
                                                     ("w", "in", "gu", "silu", "hid", "down", "out"))
        s_cq, s_ck, s_kpe, s_qp = (sem("mla_" + n) for n in ("cq", "ckv", "kpe", "qpe"))
        s_qps = sem("mla_qpe_samples")
        s_ng, s_pe, s_pn = (sem("att_" + n) for n in ("max", "exp", "p"))
        s_ckin = [sem(f"cache{i}") for i in range(2)]
        s_cn = sem("new_rows")
        t_ng, t_pe, t_pn = (sem("sam_" + n) for n in ("max", "exp", "p"))
        s_done = sem("stores")
        s_y = sem("y_stored")

        taken, used, turn = {}, [0] * 8, [0]

        def open_bank(pe, key):
            b = turn[0] % 8
            turn[0] += 1
            taken[key] = (b, used[b])
            if used[b]:
                pe.wait_ge(free[b], used[b])
            used[b] += 1
            return bank[b]

        def is_full(key):
            return full[taken[key][0]]

        def arrive(eng, key):
            b, u = taken[key]
            eng.wait_ge(full[b], u + 1)
            return bank[b]

        def is_free(key):
            return free[taken[key][0]]

        def freed(eng, key):
            b, u = taken[key]
            eng.wait_ge(free[b], u + 1)

        def slot(g):
            return ring[:, g % NSLOT, :]

        def landed(eng, g):
            eng.wait_ge(w_in[g % NSLOT], 16 * (g // NSLOT + 1))

        def experts(eng, body):
            for j in range(3):
                body(0, j)
            with eng.Fori(1, E // 3) as it:
                for j in range(3):
                    body(it, j)
            for j in range(E % 3):
                body(E // 3, j)

        def piece_turn(l, it, j, c):
            return 16 * it + 16 * ((G_MOE[l] + 3 * j + c) // NSLOT + 1)

        block = ctx.enter_context(nc.Block())
        mm = nc.tensor.matmul
        tr = nc.tensor.transpose

        @block.tensor
        def _(pe):
            pe.wait_ge(s_cst, 16)

            def sum_squares(key, src, n, base):
                ps = open_bank(pe, key)
                for k in range(n):
                    pe.wait_ge(s_sq, base + k + 1)
                    t = mm(ps[:, 0:T], ones, src[:, k, :], start=(k == 0), stop=(k == n - 1))
                t.then_inc(is_full(key), 1)

            def chunk(key, n, lhs, rhs, cols=T, wait=None):
                ps = open_bank(pe, key)
                for k in range(n):
                    if wait:
                        wait(k)
                    t = mm(ps[:, 0:cols], lhs(k), rhs(k), start=(k == 0), stop=(k == n - 1))
                t.then_inc(is_full(key), 1)

            sum_squares("n0", sq, KD, SQ["n0"])
            for c in range(KD):
                for kind in range(2):
                    g = G_PW1 + 2 * (c // 2) + kind
                    w = slot(g).rearrange("p (k f) -> p k f", k=KD)
                    landed(pe, g)

                    def wait(k):
                        if c == 0 and kind == 0:
                            pe.wait_ge(s_xn, k + 1)
                    chunk(("pw1", kind, c), KD, lambda k: w[:, k, (c % 2) * P:(c % 2 + 1) * P],
                          lambda k: xnT[:, k, :], wait=wait)
            chunk("lnm", KD, lambda k: ones, lambda k: zT[:, k, :], wait=lambda k: pe.wait_ge(s_z, k + 1))
            sum_squares("lnv", sq, KD, SQ["ln"])
            for m in range(KD):
                g = G_PW2 + m // 2
                w = slot(g).rearrange("p (k f) -> p k f", k=KD)
                landed(pe, g)
                chunk(("pw2", m), KD, lambda k: w[:, k, (m % 2) * P:(m % 2 + 1) * P], lambda k: xnT[:, k, :],
                      wait=(lambda k: pe.wait_ge(s_zs, k + 1)) if m == 0 else None)
            sum_squares("n1", sq, KD, SQ["n1"])

            def moe(l, norm):
                ps = open_bank(pe, ("router", l))
                pe.wait_ge(s_wr, 32)
                for i, (t0, n) in enumerate(TILES):
                    for k in range(KD):
                        if i == 0:
                            pe.wait_ge(s_xn, KD * norm + k + 1)
                        t = mm(ps[0:n, i * (G + E):(i + 1) * (G + E)], xnT[:, k, t0:t0 + n], wr[:, l, k, :],
                               start=(k == 0), stop=(k == KD - 1))
                t.then_inc(is_full(("router", l)), 1)
                for i, (t0, n) in enumerate(TILES):
                    for hf in range(2):
                        ps = open_bank(pe, ("row", l, i, hf))
                        for k in range(4):
                            t = tr(ps[0:n, k * P:(k + 1) * P], xnT[:, 4 * hf + k, t0:t0 + n], ident)
                        t.then_inc(is_full(("row", l, i, hf)), 1)
                ps = open_bank(pe, ("rank", l))
                pe.wait_ge(s_hot, l + 1)
                M = rt["M"]
                for i, (t0, n) in enumerate(TILES):
                    for b in range(i + 1):
                        m = TILES[b][1]
                        mm(ps[0:n, i * E:(i + 1) * E], (tri if b == i else ones)[0:m, 0:n], M[0:m, b, :],
                           start=(b == 0), stop=(b == i))
                for b in range(3):
                    m = TILES[b][1]
                    t = mm(ps[:, 3 * E:4 * E], ones[0:m, :], M[0:m, b, :], start=(b == 0), stop=(b == 2))
                t.then_inc(is_full(("rank", l)), 1)
                for i in range(3):
                    for hf in range(2):
                        freed(pe, ("row", l, i, hf))
                for hf in range(2):
                    for k in range(KD):
                        ps = open_bank(pe, ("xg", l, hf, k))
                        for i, (t0, n) in enumerate(TILES):
                            if hf == 0 and k == 0:
                                pe.wait_ge(s_S, 3 * l + i + 1)
                            t = mm(ps[:, 0:HALF], XR[0:n, i, k:D:KD], S[0:n, i, hf * HALF:(hf + 1) * HALF],
                                   start=(i == 0), stop=(i == 2))
                        t.then_inc(is_full(("xg", l, hf, k)), 1)
                for b in range(6):
                    if used[b]:
                        pe.wait_ge(free[b], used[b])
                eb = E * l

                def gate_up(it, j):
                    e = 3 * it + j
                    pe.wait_ge(s_xe, e + (eb + 1))
                    if not isinstance(it, int) or it:
                        pe.wait_ge(s_hid, e + (eb - 2))
                    for c in range(2):
                        g = G_MOE[l] + 3 * j + c
                        pe.wait_ge(w_in[g % NSLOT], piece_turn(l, it, j, c))
                        w = slot(g).rearrange("p (k f) -> p k f", k=KD)
                        for m in range(FK):
                            o = bank[j][:, (2 * c + m) * W:(2 * c + m + 1) * W]
                            for k in range(KD):
                                t = mm(o, w[:, k, m * P:(m + 1) * P], xe[:, j, k, :], start=(k == 0),
                                       stop=(k == KD - 1))
                    t.then_inc(s_gu, 1)

                def down(it, j, warm):
                    e = 3 * it + j
                    pe.wait_ge(s_hid, e + (eb + 1))
                    if warm:
                        pe.wait_ge(s_out, e + (eb - 2))
                    g = G_MOE[l] + 3 * j + 2
                    pe.wait_ge(w_in[g % NSLOT], piece_turn(l, it, j, 2))
                    w = slot(g).rearrange("p (k f) -> p k f", k=FK)
                    for m in range(KD):
                        for k in range(FK):
                            t = mm(bank[3 + j][:, m * W:(m + 1) * W], w[:, k, m * P:(m + 1) * P], hid[:, j, k, :],
                                   start=(k == 0), stop=(k == FK - 1))
                    t.then_inc(s_dn, 1)

                gate_up(0, 0)
                gate_up(0, 1)
                down(0, 0, False)
                gate_up(0, 2)
                down(0, 1, False)
                gate_up(1, 0)
                down(0, 2, False)
                gate_up(1, 1)
                down(1, 0, True)
                gate_up(1, 2)
                down(1, 1, True)
                with pe.Fori(2, E // 3) as it:
                    gate_up(it, 0)
                    down(it - 1, 2, True)
                    gate_up(it, 1)
                    down(it, 0, True)
                    gate_up(it, 2)
                    down(it, 1, True)
                gate_up(E // 3, 0)
                down(E // 3 - 1, 2, True)
                gate_up(E // 3, 1)
                down(E // 3, 0, True)
                down(E // 3, 1, True)
                pe.wait_ge(s_off, l + 1)
                with pe.If(pe.value_load(mostI[0:1, 0:1], min_val=0, max_val=NPAIR) > W):
                    pe.wait_ge(s_hid, eb + E)
                    pe.wait_ge(s_out, eb + E)
                    with pe.Fori(0, E) as e:
                        for k4 in range(NXW):
                            pe.wait_ge(x_w[l], 48 * e + 48)
                            pe.wait_ge(x_xe[l], NXW * e + (k4 + 1))
                            for c in range(2):
                                w = exw[:, c, :].rearrange("p (k f) -> p k f", k=KD)
                                for m in range(FK):
                                    for k in range(KD):
                                        t = mm(bank[0][:, (2 * c + m) * W:(2 * c + m + 1) * W],
                                               w[:, k, m * P:(m + 1) * P], xe[:, 0, k, :], start=(k == 0),
                                               stop=(k == KD - 1))
                            t.then_inc(x_gu[l], 1)
                            pe.wait_ge(x_hid[l], NXW * e + (k4 + 1))
                            w = exw[:, 2, :].rearrange("p (k f) -> p k f", k=FK)
                            for m in range(KD):
                                for k in range(FK):
                                    t = mm(bank[3][:, m * W:(m + 1) * W], w[:, k, m * P:(m + 1) * P], hid[:, 0, k, :],
                                           start=(k == 0), stop=(k == FK - 1))
                            t.then_inc(x_dn[l], 1)
                pe.wait_ge(s_SG, 3 * (l + 1))
                pe.wait_ge(s_mo, l + 1)
                for i in range(NST):
                    n = min(P, NPAIR - i * P)
                    ps = open_bank(pe, ("gm", l, i))
                    for b, (t0, m) in enumerate(TILES):
                        t = tr(ps[0:n, t0:t0 + m], SG[0:m, b, i * P:i * P + n], ident[0:m, 0:m])
                    t.then_inc(is_full(("gm", l, i)), 1)
                for i in range(NST):
                    n = min(P, NPAIR - i * P)
                    for hf in range(2):
                        ps = open_bank(pe, ("or", l, i, hf))
                        for k in range(4):
                            t = tr(ps[0:n, k * P:(k + 1) * P], OutT[:, 4 * hf + k, i * P:i * P + n], ident)
                        t.then_inc(is_full(("or", l, i, hf)), 1)
                for i in range(NST):
                    freed(pe, ("gm", l, i))
                for k in range(KD):
                    ps = open_bank(pe, ("mo", l, k))
                    for i in range(NST):
                        n = min(P, NPAIR - i * P)
                        if k in (0, 4):
                            freed(pe, ("or", l, i, k // 4))
                        t = mm(ps[:, 0:T], OutR[0:n, i, k * P:(k + 1) * P], Gm[0:n, i, :], start=(i == 0),
                               stop=(i == NST - 1))
                    t.then_inc(is_full(("mo", l, k)), 1)

            def embed(l, norm):
                pe.wait_ge(s_p, 16)
                win = slot(G_PLE[l]).rearrange("p (k f) -> p k f", k=2)
                for m in range(KD):
                    g = G_PLE[l] + 1 + m // 2
                    w = slot(g).rearrange("p (k f) -> p k f", k=KD)
                    landed(pe, g)
                    chunk(("pg", l, m), KD, lambda k: w[:, k, (m % 2) * P:(m % 2 + 1) * P], lambda k: xnT[:, k, :],
                          wait=(lambda k: pe.wait_ge(s_xn, KD * norm + k + 1)) if m == 0 else None)
                    landed(pe, G_PLE[l])
                    chunk(("pin", l, m), 2, lambda k: win[:, k, m * P:(m + 1) * P], lambda k: pT[:, l, k, :])

            moe(0, 1)
            sum_squares("n2", sq, KD, SQ["n2"])
            embed(0, 2)
            sum_squares("n3", sq, KD, SQ["n3"])

            def dkv(k):
                return slot(G_DKV + k // 4)[:, 0:4 * (KL + P)].rearrange("p (k f) -> p k f", k=4)[:, k % 4, :]

            def dq(k):
                return slot(G_DQ + k // 4)[:, 0:4 * QL].rearrange("p (k f) -> p k f", k=4)[:, k % 4, :]

            for g in (G_DQ, G_DQ + 1, G_DKV, G_DKV + 1):
                landed(pe, g)
            for m in range(KQ):
                chunk(("cq", m), KD, lambda k: dq(k)[:, m * P:(m + 1) * P], lambda k: xnT[:, k, :],
                      wait=(lambda k: pe.wait_ge(s_xn, KD * 3 + k + 1)) if m == 0 else None)
            for m in range(KK):
                chunk(("kv", m), KD, lambda k: dkv(k)[:, m * P:(m + 1) * P], lambda k: xnT[:, k, :])
            chunk("kpe", KD, lambda k: dkv(k)[:, KL:KL + P], lambda k: xnT[:, k, :])
            sum_squares("q", sq, KQ, SQ["q"])
            sum_squares("kv", sq[:, KQ:KQ + KK, :], KK, SQ["kv"])
            freed(pe, "kpe")
            chunk("krot", 1, lambda k: cst[:, C_ROT:C_ROT + P], lambda k: kr)
            uq = [slot(G_UQ + k) for k in range(KQ)]
            for k in range(KQ):
                landed(pe, G_UQ + k)
            for c in range(4):
                chunk(("qp", c), KQ, lambda k: uq[k][:, H * DN + c * P:H * DN + (c + 1) * P], lambda k: cqT[:, k, :],
                      wait=(lambda k: pe.wait_ge(s_cq, k + 1)) if c == 0 else None)
            for c in range(4):
                for m in (2 * c, 2 * c + 1):
                    chunk(("qn", m), KQ, lambda k: uq[k][:, m * P:(m + 1) * P], lambda k: cqT[:, k, :])
                freed(pe, ("qp", c))
                chunk(("qrot", c), 1, lambda k: cst[:, C_ROT:C_ROT + P], lambda k: qpr[:, c, :])
            landed(pe, G_UK)
            landed(pe, G_UV)
            uk = slot(G_UK).rearrange("p (k f) -> p k f", k=KK)
            uv = slot(G_UV).rearrange("p (k f) -> p k f", k=KK)
            for c in range(KD):
                chunk(("kn", c), KK, lambda k: uk[:, k, c * P:(c + 1) * P], lambda k: ckvT[:, k, 0:TP], cols=TP,
                      wait=(lambda k: pe.wait_ge(s_ck, k + 1)) if c == 0 else None)
            for i in range(2):
                for hf in range(2):
                    chunk(("V", i, hf), KK, lambda k: ckvT[:, k, i * P:(i + 1) * P],
                          lambda k: uv[:, k, hf * 512:(hf + 1) * 512], cols=512)
            ps = open_bank(pe, "ckr")
            for k in range(KK):
                t = tr(ps[0:TS, k * P:(k + 1) * P], ckvT[:, k, TP:T], ident)
            t.then_inc(is_full("ckr"), 1)
            pe.wait_ge(s_uk, 16)
            for m in range(KD):
                freed(pe, ("qn", m))
            for odd in range(2):
                ps = open_bank(pe, ("ql", odd))
                r = slice(DN * odd, DN * odd + DN)
                for c in range(KD):
                    for k in range(KK):
                        t = mm(ps[:, (k * KD + c) * TS:(k * KD + c + 1) * TS], wukT[r, c, k * P:(k + 1) * P],
                               qnT[r, c, TP:T], start=True, stop=True)
                t.then_inc(is_full(("ql", odd)), 1)

            def scores(h):
                ps = open_bank(pe, ("sc", h))
                c, r = h // 2, slice(DN * (h % 2), DN * (h % 2) + DN)
                c4, r4 = h // 4, slice(DR * (h % 4), DR * (h % 4) + DR)
                if h == 0:
                    for m in range(KD):
                        freed(pe, ("kn", m))
                if h % 4 == 0:
                    pe.wait_ge(s_qp, h // 4 + 1)
                for i in range(2):
                    o = ps[:, P * i:P * i + P * (i + 1)]
                    mm(o, qnT[r, c, i * P:(i + 1) * P], knT[r, c, 0:(i + 1) * P], start=True, stop=False)
                    t = mm(o, qpeT[r4, c4, i * P:(i + 1) * P], kpeT[r4, 0:(i + 1) * P], start=False, stop=True)
                t.then_inc(is_full(("sc", h)), 1)

            def turn_weights(h):
                ps = open_bank(pe, ("pt", h))
                pe.wait_ge(s_pn, h + 1)
                for k in range(3):
                    t = tr(ps[:, k * P:(k + 1) * P], pr[:, h % 2, k * P:(k + 1) * P], ident)
                t.then_inc(is_full(("pt", h)), 1)

            def values(h):
                c, r = h // 2, slice(DV * (h % 2), DV * (h % 2) + DV)
                if h % 2 == 0:
                    open_bank(pe, ("o", c))
                ps = bank[taken[("o", c)][0]]
                freed(pe, ("pt", h))
                if h == 0:
                    for i in range(2):
                        for hf in range(2):
                            freed(pe, ("V", i, hf))
                v = [V[:, i, h * DV:(h + 1) * DV] for i in range(2)]
                mm(ps[r, 0:P], v[0], PT[:, h % 4, 0:P], start=True, stop=True)
                mm(ps[r, P:2 * P], v[0], PT[:, h % 4, P:2 * P], start=True, stop=False)
                t = mm(ps[r, P:2 * P], v[1], PT[:, h % 4, 2 * P:3 * P], start=False, stop=True)
                if h % 2:
                    t.then_inc(is_full(("o", c)), 1)

            for i in range(H + 2):
                if i < H:
                    scores(i)
                if 1 <= i <= H:
                    turn_weights(i - 1)
                if i >= 2:
                    values(i - 2)

            def sample_scores(b):
                if b == 0:
                    freed(pe, ("ql", 0))
                    freed(pe, ("ql", 1))
                    pe.wait_ge(s_qps, 4)
                pe.wait_ge(s_ckin[b % 2], 48 * PAGES * (b // 2 + 1))
                for q2 in range(3):
                    ps = open_bank(pe, ("ss", b, q2))
                    n = 512 if q2 < 2 else 1
                    for k in range(KK):
                        mm(ps[0:H, 0:n], qlat[:, k, b, :],
                           CKT[b % 2][:, 4 * q2:4 * q2 + 4, k, :] if q2 < 2 else ckvT[:, k, TP + b:TP + b + 1],
                           start=(k == 0), stop=False)
                    t = mm(ps[0:H, 0:n], qps[0:DR, b, :],
                           KPT[0:DR, b % 2, q2 * 512:(q2 + 1) * 512] if q2 < 2 else kpeT[0:DR, TP + b:TP + b + 1],
                           start=False, stop=True)
                    t.then_inc(is_full(("ss", b, q2)), 1)

            def sample_weights(b):
                ps = open_bank(pe, ("sp", b))
                pe.wait_ge(t_pn, b + 1)
                for g in range(PAGES):
                    tr(ps[:, g * H:(g + 1) * H], pp[0:H, g * P:(g + 1) * P], ident[0:H, 0:H])
                tr(ps[0:1, PAGES * H:(PAGES + 1) * H], pp[0:H, PAST:PAST + 1],
                   ident[0:H, 0:H]).then_inc(is_full(("sp", b)), 1)

            def sample_values(b):
                ps = open_bank(pe, ("sv", b))
                freed(pe, ("sp", b))
                if b == 0:
                    pe.wait_ge(s_cn, 16)
                ck = CK[:, b % 2, :].rearrange("p (g f) -> p g f", g=PAGES)
                for k in range(KK):
                    for g in range(PAGES):
                        mm(ps[:, k * H:(k + 1) * H], ck[:, g, k * P:(k + 1) * P], PTs[:, g, :], start=(g == 0),
                           stop=False)
                    t = mm(ps[:, k * H:(k + 1) * H], CN[0:1, b, k * P:(k + 1) * P], PTs[0:1, PAGES, :],
                           start=False, stop=True)
                t.then_inc(is_full(("sv", b)), 1)

            sample_scores(0)
            for b in range(TS):
                if b + 1 < TS:
                    sample_scores(b + 1)
                sample_weights(b)
                sample_values(b)
            ps = open_bank(pe, "so")
            for b in range(TS):
                freed(pe, ("sv", b))
            for h in range(H):
                c, r = h // 2, slice(DV * (h % 2), DV * (h % 2) + DV)
                for k in range(KK):
                    t = mm(ps[r, c * TS:(c + 1) * TS], uv[:, k, h * DV:(h + 1) * DV], olat[:, k, h, :],
                           start=(k == 0), stop=(k == KK - 1))
            t.then_inc(is_full("so"), 1)
            freed(pe, "so")
            for c in range(KD):
                freed(pe, ("o", c))
            for m in range(KD):
                g = G_WO + m // 2
                w = slot(g).rearrange("p (k f) -> p k f", k=KD)
                landed(pe, g)
                chunk(("wo", m), KD, lambda k: w[:, k, (m % 2) * P:(m % 2 + 1) * P], lambda k: oT[:, k, :])
            sum_squares("n4", sq, KD, SQ["n4"])
            moe(1, 4)
            sum_squares("n5", sq, KD, SQ["n5"])
            embed(1, 5)
            sum_squares("n6", sq, KD, SQ["n6"])

        v, s = nc.vector, nc.scalar

        def vcol(name, k):
            return vt[:, VCOL[name] + k:VCOL[name] + k + 1]

        @block.vector
        def _(dve):
            steps = [0]

            def step(ins):
                steps[0] += 1
                ins.then_inc(s_dve, 1)
                dve.wait_ge(s_dve, steps[0])

            def inverse_root(key, n):
                ps = arrive(dve, key)
                v.tensor_scalar(rstd[:], ps[:, 0:T], 1.0 / n, EPS, ALU.mult, ALU.add).then_inc(is_free(key), 1)
                dve.wait_ge(s_rs, NORMS.index(key) + 1)
                step(v.reciprocal(rstd[:], rstd[:]))

            def norm(key, gain, col):
                inverse_root(key, D)
                for k in range(KD):
                    v.scalar_tensor_tensor(out=xnT[:, k, :], in0=hT[:, k, :], scalar=vcol(gain, col + k), in1=rstd[:],
                                           op0=ALU.mult, op1=ALU.mult).then_inc(s_xn, 1)

            def add_to_h(key, k):
                ps = arrive(dve, key)
                v.tensor_tensor(hT[:, k, :], hT[:, k, :], ps[:, 0:T], ALU.add).then_inc(is_free(key), 1)

            dve.wait_ge(s_x, 16)
            dve.wait_ge(s_vec, 16)
            norm("n0", "norm_mix", 0)
            dve.wait_ge(s_dw, 16)
            dve.wait_ge(s_st, 16)
            dve.wait_ge(s_zero, 1)
            cv = 0
            tap = wdw[:].rearrange("p (j k) -> p k j", k=KD)
            for c2 in range(KD // 2):
                for c in (2 * c2, 2 * c2 + 1):
                    key = ("pw1", 0, c)
                    ps = arrive(dve, key)
                    freed(dve, ("pw1", 1, c))
                    step(v.scalar_tensor_tensor(out=uT[:, c, CW - 1:CW - 1 + TP], in0=ps[:, 0:TP],
                                                scalar=vcol("conv_b_pw1", c), in1=sgu[:, c % 2, 0:TP], op0=ALU.add,
                                                op1=ALU.mult))
                    v.scalar_tensor_tensor(out=stT[:, c, :, CW - 1], in0=ps[:, TP:T], scalar=vcol("conv_b_pw1", c),
                                           in1=sgu[:, c % 2, TP:T], op0=ALU.add, op1=ALU.mult)\
                     .then_inc(is_free(key), 1)
                for c in (2 * c2, 2 * c2 + 1):
                    freed(dve, ("pw1", 0, c))
                    v.tensor_scalar(zT[:, c, 0:TP], uT[:, c, 0:TP], wdw[:, c:c + 1], vcol("conv_b_dw", c), ALU.mult,
                                    ALU.add).then_inc(s_cv, 1)
                    cv += 1
                for j in range(1, CW):
                    for c in (2 * c2, 2 * c2 + 1):
                        dve.wait_ge(s_cv, cv - 1)
                        v.scalar_tensor_tensor(out=zT[:, c, 0:TP], in0=uT[:, c, j:j + TP],
                                               scalar=wdw[:, j * KD + c:j * KD + c + 1], in1=zT[:, c, 0:TP],
                                               op0=ALU.mult, op1=ALU.add).then_inc(s_cv, 1)
                        cv += 1
                for c in (2 * c2, 2 * c2 + 1):
                    dve.wait_ge(s_cv, cv)
                    step(v.tensor_tensor(ctmp, stT[:, c, :, :], tap[:, c, :].unsqueeze(1).to_broadcast([P, TS, CW]),
                                         ALU.mult))
                    step(v.reduce_sum(zT[:, c, TP:T], ctmp, AX.X))
                    v.tensor_scalar(zT[:, c, TP:T], zT[:, c, TP:T], vcol("conv_b_dw", c), None, ALU.add)\
                     .then_inc(s_z, 1)
            ps = arrive(dve, "lnm")
            v.tensor_scalar(mu, ps[:, 0:T], 1.0 / D, None, ALU.mult).then_inc(is_free("lnm"), 1)
            freed(dve, "lnm")
            dve.wait_ge(s_z, KD)
            for k in range(KD):
                v.tensor_tensor(zT[:, k, :], zT[:, k, :], mu, ALU.subtract).then_inc(s_zc, 1)
            inverse_root("lnv", D)
            for k in range(KD):
                v.tensor_tensor(zT[:, k, :], zT[:, k, :], rstd[:], ALU.mult).then_inc(s_zn, 1)
            for m in range(KD):
                add_to_h(("pw2", m), m)
            for m in range(KD):
                freed(dve, ("pw2", m))
            norm("n1", "norm_ffn", 0)

            def route(l):
                L, gl8, gmx, em, G32, emx, M1, M2, M, pos, ex, eidx, gidx, gsum, den, w1, w2, slot1, slot2 = (
                    rt[n] for n in ("L", "gl8", "gmx", "em", "G32", "emx", "M1", "M2", "M", "pos", "ex", "eidx", "gidx",
                                    "gsum", "den", "w1", "w2", "slot1", "slot2"))
                iota = cst[:, C_IOTA:C_IOTA + NPAIR]
                n3 = G + E
                key = ("router", l)
                ps = arrive(dve, key)
                dve.wait_ge(s_wr, 32)
                dve.wait_ge(s_zero, 4)
                step(v.tensor_tensor(L[:, 0:2, :], ps[:, 0:2 * n3].rearrange("p (i e) -> p i e", i=2),
                                     br[:, l, :].unsqueeze(1).to_broadcast([P, 2, n3]), ALU.add))
                v.tensor_tensor(L[0:TS, 2, :], ps[0:TS, 2 * n3:3 * n3], br[0:TS, l, :], ALU.add)\
                 .then_inc(is_free(key), 1)
                freed(dve, key)
                step(v.tensor_copy(gl8[:, :, 0:G], L[:, :, 0:G]))
                for i in range(3):
                    last = v.max(gmx[:, i, :], gl8[:, i, :])
                step(last)
                for i in range(3):
                    last = v.max_index(gix[:, i, :], gmx[:, i, :], gl8[:, i, :])
                step(last)
                step(v.tensor_copy(gidx[:], gix[:, :, 0:1]))
                step(v.tensor_tensor(G32[:], cst[:, C_GRP:C_GRP + E].unsqueeze(1).to_broadcast([P, 3, E]),
                                     gidx[:].to_broadcast([P, 3, E]), ALU.is_equal))
                step(v.tensor_tensor(em[:], L[:, :, G:n3], G32[:], ALU.mult))
                step(v.tensor_scalar(pos[:], G32[:], BIG, -BIG, ALU.mult, ALU.add))
                step(v.tensor_tensor(em[:], em[:], pos[:], ALU.add))
                for i in range(3):
                    last = v.max(emx[:, i, :], em[:, i, :])
                step(last)
                for i in range(3):
                    last = v.max_index(eix[:, i, :], emx[:, i, :], em[:, i, :])
                step(last)
                step(v.tensor_copy(eidx[:], eix[:, :, 0:2]))
                io = cst[:, C_IOTA:C_IOTA + E].unsqueeze(1).to_broadcast([P, 3, E])
                v.tensor_tensor(M1[:], io, eidx[:, :, 0:1].to_broadcast([P, 3, E]), ALU.is_equal)
                step(v.tensor_tensor(M2[:], io, eidx[:, :, 1:2].to_broadcast([P, 3, E]), ALU.is_equal))
                v.tensor_tensor(M[:], M1[:], M2[:], ALU.add).then_inc(s_hot, 1)
                v.tensor_tensor(ex[:, :, 0:G], gl8[:, :, 0:G], gmx[:, :, 0:1].to_broadcast([P, 3, G]), ALU.subtract)
                v.tensor_tensor(ex[:, :, G:G + 1], emx[:, :, 1:2], emx[:, :, 0:1], ALU.subtract).then_inc(s_pre, 1)
                key = ("rank", l)
                ps = arrive(dve, key)
                step(v.tensor_copy(cnt[:], ps[:, 3 * E:4 * E]))
                step(v.tensor_tensor_scan(incl[:], ones[:, 0:E], cnt[:], 0.0, ALU.mult, ALU.add))
                step(v.tensor_tensor(off[:], incl[:], cnt[:], ALU.subtract))
                step(v.tensor_tensor(pos[:, 0:2, :], ps[:, 0:2 * E].rearrange("p (i e) -> p i e", i=2),
                                     off[:].unsqueeze(1).to_broadcast([P, 2, E]), ALU.add))
                v.tensor_tensor(pos[0:TS, 2, :], ps[0:TS, 2 * E:3 * E], off[0:TS, :], ALU.add)\
                 .then_inc(is_free(key), 1)
                freed(dve, key)
                step(v.tensor_tensor(em[:], M1[:], pos[:], ALU.mult))
                step(v.reduce_sum(slot1[:], em[:], AX.X))
                step(v.tensor_tensor(em[:], M2[:], pos[:], ALU.mult))
                v.reduce_sum(slot2[:], em[:], AX.X).then_inc(s_slot, 1)
                dve.wait_ge(s_slot, l + 1)
                for i, (t0, n) in enumerate(TILES):
                    step(v.tensor_scalar(S[0:n, i, :], iota[0:n, :], slot1[0:n, i, :], None, ALU.is_equal))
                    v.scalar_tensor_tensor(out=S[0:n, i, :], in0=iota[0:n, :], scalar=slot2[0:n, i, :],
                                           in1=S[0:n, i, :], op0=ALU.is_equal, op1=ALU.add).then_inc(s_S, 1)
                dve.wait_ge(s_ex, l + 1)
                step(v.reduce_sum(gsum[:], ex[:, :, 0:G], AX.X))
                step(v.tensor_scalar(den[:], ex[:, :, G:G + 1], 1.0, None, ALU.add))
                step(v.tensor_tensor(den[:], den[:], gsum[:], ALU.mult))
                step(v.reciprocal(w1[:], den[:]))
                v.tensor_tensor(w2[:], w1[:], ex[:, :, G:G + 1], ALU.mult).then_inc(s_w, 1)
                step(v.tensor_copy(offI[:], off[:]))
                step(v.reduce_max(most[:], cnt[:], AX.X))
                step(v.tensor_copy(mostI[:], most[:]))
                w64 = cst[:, C_W64:C_W64 + NXW * E].rearrange("p (w e) -> p w e", w=NXW)

                def wide(x):
                    return x[:].unsqueeze(1).to_broadcast([P, NXW, E])
                step(v.tensor_tensor(xfl[:], wide(cnt), w64, ALU.is_gt))
                step(v.tensor_tensor(xst[:], wide(off), w64, ALU.add))
                step(v.tensor_scalar(incl[:], incl[:], -float(W), None, ALU.add))
                step(v.tensor_tensor(xst[:], xst[:], wide(incl), ALU.min))
                step(v.tensor_scalar(xst[:], xst[:], -float(NPAIR), None, ALU.add))
                step(v.tensor_tensor(xst[:], xst[:], xfl[:], ALU.mult))
                step(v.tensor_scalar(xst[:], xst[:], float(NPAIR), None, ALU.add))
                v.tensor_copy(xstI[:], xst[:]).then_inc(s_off, 1)

            def moe(l):
                route(l)
                for hf in range(2):
                    for k in range(1, KD, 2):
                        key = ("xg", l, hf, k)
                        ps = arrive(dve, key)
                        v.tensor_copy(XGT[:, k, hf * HALF:(hf + 1) * HALF], ps[:, 0:HALF]).then_inc(is_free(key), 1)
                for hf in range(2):
                    for k in range(KD):
                        freed(dve, ("xg", l, hf, k))
                dve.wait_ge(s_pad, l + 1)
                dve.wait_ge(s_off, l + 1)
                eb = E * l

                def window_in(it, j):
                    e = 3 * it + j
                    at = dve.value_load(offI[0:1, bass.ds(e, 1)], min_val=0, max_val=NPAIR)
                    if not isinstance(e, int) or e >= 3:
                        dve.wait_ge(s_gu, e + (eb - 2))
                    v.tensor_copy(xe[:, j % 3, :, :], XGT[:, :, bass.ds(at, W)]).then_inc(s_xe, 1)

                def body(it, j):
                    e = 3 * it + j
                    if not isinstance(e, int) or e + 2 < E:
                        window_in(it, j + 2)
                    dve.wait_ge(s_sg, e + (eb + 1))
                    if not isinstance(e, int) or e >= 3:
                        dve.wait_ge(s_dn, e + (eb - 2))
                    v.tensor_tensor(hid[:, j, :, :], sg[:, j, :, :],
                                    bank[j][:, FK * W:2 * FK * W].rearrange("p (m w) -> p m w", m=FK), ALU.mult)\
                     .then_inc(s_hid, 1)

                window_in(0, 0)
                window_in(0, 1)
                experts(dve, body)
                with dve.If(dve.value_load(mostI[0:1, 0:1], min_val=0, max_val=NPAIR) > W):
                    dve.wait_ge(s_gu, eb + E)
                    dve.wait_ge(s_dn, eb + E)
                    with dve.Fori(0, E) as e:
                        for q in range(NXW):
                            at = dve.value_load(xstI[0:1, q, bass.ds(e, 1)], min_val=0, max_val=NPAIR)
                            dve.wait_ge(x_out[l], NXW * e + (q + 1))
                            v.tensor_copy(xe[:, 0, :, :], XGT[:, :, bass.ds(at, W)]).then_inc(x_xe[l], 1)
                            dve.wait_ge(x_sg[l], NXW * e + (q + 1))
                            v.tensor_tensor(hid[:, 0, :, :], sg[:, 0, :, :],
                                            bank[0][:, FK * W:2 * FK * W].rearrange("p (m w) -> p m w", m=FK),
                                            ALU.mult).then_inc(x_hid[l], 1)
                for i in range(NST):
                    n = min(P, NPAIR - i * P)
                    key = ("gm", l, i)
                    ps = arrive(dve, key)
                    v.tensor_copy(Gm[0:n, i, :], ps[0:n, 0:T]).then_inc(is_free(key), 1)
                for i in range(NST):
                    n = min(P, NPAIR - i * P)
                    key = ("or", l, i, 1)
                    ps = arrive(dve, key)
                    v.tensor_copy(OutR[0:n, i, 512:1024], ps[0:n, :]).then_inc(is_free(key), 1)
                for k in range(KD):
                    add_to_h(("mo", l, k), k)
                for k in range(KD):
                    freed(dve, ("mo", l, k))

            def embed(l):
                for m in range(KD):
                    key = ("pin", l, m)
                    ps = arrive(dve, key)
                    freed(dve, ("pg", l, m))
                    v.tensor_tensor(tgp[:, m % 2, :], sgp[:, m % 2, :], ps[:, 0:T], ALU.mult)\
                     .then_inc(is_free(key), 1)
                    freed(dve, key)
                    v.tensor_tensor(hT[:, m, :], hT[:, m, :], tgp[:, m % 2, :], ALU.add).then_inc(s_ple, 1)
                dve.wait_ge(s_ple, KD * (l + 1))

            dve.wait_ge(s_done, 32)
            moe(0)
            norm("n2", "ple_g", 0)
            embed(0)
            norm("n3", "norm_mix", KD)
            for m in range(KQ):
                ps = arrive(dve, ("cq", m))
                v.tensor_copy(cqr[:, m, :], ps[:, 0:T]).then_inc(is_free(("cq", m)), 1)
            for m in range(KK):
                ps = arrive(dve, ("kv", m))
                v.tensor_copy(kvr[:, m, :], ps[:, 0:T]).then_inc(is_free(("kv", m)), 1)
            for m in range(KQ):
                freed(dve, ("cq", m))
            for m in range(KK):
                freed(dve, ("kv", m))
            inverse_root("q", QL)
            for k in range(KQ):
                v.scalar_tensor_tensor(out=cqT[:, k, :], in0=cqr[:, k, :], scalar=vcol("mla_g_q", k), in1=rstd[:],
                                       op0=ALU.mult, op1=ALU.mult).then_inc(s_cq, 1)
            dve.wait_ge(s_cq, KQ)
            inverse_root("kv", KL)
            for k in range(KK):
                v.scalar_tensor_tensor(out=ckvT[:, k, :], in0=kvr[:, k, :], scalar=vcol("mla_g_kv", k), in1=rstd[:],
                                       op0=ALU.mult, op1=ALU.mult).then_inc(s_ck, 1)
            cos, sin = cst[:, C_COS:C_COS + T], cst[:, C_SIN:C_SIN + T]

            def rotate(key, raw, out, done):
                ps = arrive(dve, key)
                step(v.tensor_tensor(rtmp[:, 0, :], raw, cos, ALU.mult))
                v.tensor_tensor(rtmp[:, 1, :], ps[:, 0:T], sin, ALU.mult).then_inc(is_free(key), 1)
                freed(dve, key)
                v.tensor_tensor(out, rtmp[:, 0, :], rtmp[:, 1, :], ALU.add).then_inc(done, 1)

            freed(dve, "kpe")
            rotate("krot", kr, kpeT, s_kpe)
            dve.wait_ge(s_kpe, 1)
            for c in range(4):
                freed(dve, ("qp", c))
                rotate(("qrot", c), qpr[:, c, :], qpeT[:, c, :], s_qp)
                dve.wait_ge(s_qp, c + 1)
            for c in range(KD):
                ps = arrive(dve, ("kn", c))
                v.tensor_copy(knT[:, c, :], ps[:, 0:TP]).then_inc(is_free(("kn", c)), 1)
            for g in range(4):
                v.tensor_copy(qps[0:DR, :, g:H:4], qpeT[g * DR:(g + 1) * DR, :, TP:T].rearrange("p c b -> p b c"))\
                 .then_inc(s_qps, 1)
            for odd in range(2):
                key = ("ql", odd)
                ps = arrive(dve, key)
                v.tensor_copy(qlat[:, :, :, odd:H:2].rearrange("p k b c -> p k c b"),
                              ps[:, 0:KK * KD * TS].rearrange("p (k c b) -> p k c b", k=KK, c=KD))\
                 .then_inc(is_free(key), 1)

            nmx = stat[:, 0:2 * H]
            esum = stat[:, 2 * H:4 * H]
            rinv = stat[:, 4 * H:6 * H]

            def head_max(h):
                key = ("sc", h)
                ps = arrive(dve, key)
                if h >= 2:
                    dve.wait_ge(s_pe, h - 1)
                v.scalar_tensor_tensor(out=sS[:, h % 2, :], in0=ps[:, 0:384], scalar=SCALE,
                                       in1=cst[:, C_MASK:C_MASK + 384], op0=ALU.mult, op1=ALU.add)\
                 .then_inc(is_free(key), 1)
                freed(dve, key)
                v.tensor_reduce(nmx[:, 2 * h:2 * h + 1], sS[:, h % 2, 0:P], AX.X, ALU.max, negate=True)
                v.tensor_reduce(nmx[:, 2 * h + 1:2 * h + 2], sS[:, h % 2, P:384], AX.X, ALU.max, negate=True)\
                 .then_inc(s_ng, 1)

            def head_norm(h):
                dve.wait_ge(s_pe, h + 1)
                step(v.reciprocal(rinv[:, 2 * h:2 * h + 2], esum[:, 2 * h:2 * h + 2]))
                v.tensor_scalar(pr[:, h % 2, 0:P], pr[:, h % 2, 0:P], rinv[:, 2 * h:2 * h + 1], None, ALU.mult)
                v.tensor_scalar(pr[:, h % 2, P:384], pr[:, h % 2, P:384], rinv[:, 2 * h + 1:2 * h + 2], None,
                                ALU.mult).then_inc(s_pn, 1)

            def head_out(c):
                ps = arrive(dve, ("o", c))
                v.tensor_copy(oT[:, c, 0:TP], ps[:, 0:TP]).then_inc(is_free(("o", c)), 1)

            for i in range(H + 2):
                if i < H:
                    head_max(i)
                if 1 <= i <= H:
                    head_norm(i - 1)
                if i >= 3 and i % 2 == 1:
                    head_out((i - 3) // 2)
            for c in range(KD):
                if (H + 1 - 3) // 2 < c:
                    head_out(c)

            for b in range(TS):
                for q2 in range(3):
                    freed(dve, ("ss", b, q2))
                v.tensor_reduce(sstat[0:H, b:b + 1], sc[0:H, :], AX.X, ALU.max, negate=True).then_inc(t_ng, 1)
                dve.wait_ge(t_pe, b + 1)
                step(v.reciprocal(sstat[0:H, 16 + b:17 + b], sstat[0:H, 8 + b:9 + b]))
                v.tensor_scalar(pp[0:H, :], pp[0:H, :], sstat[0:H, 16 + b:17 + b], None, ALU.mult).then_inc(t_pn, 1)
                key = ("sp", b)
                ps = arrive(dve, key)
                step(v.tensor_copy(PTs[:, 0:PAGES, :], ps[:, 0:PAGES * H].rearrange("p (g h) -> p g h", g=PAGES)))
                v.tensor_copy(PTs[0:1, PAGES, :], ps[0:1, PAGES * H:(PAGES + 1) * H]).then_inc(is_free(key), 1)
                key = ("sv", b)
                ps = arrive(dve, key)
                v.tensor_copy(olat[:, :, :, b], ps[:, 0:KK * H].rearrange("p (k h) -> p k h", k=KK))\
                 .then_inc(is_free(key), 1)
            ps = arrive(dve, "so")
            v.tensor_copy(oT[:, :, TP:T], ps[:, 0:KD * TS].rearrange("p (c b) -> p c b", c=KD))\
             .then_inc(is_free("so"), 1)
            for m in range(KD):
                add_to_h(("wo", m), m)
            for m in range(KD):
                freed(dve, ("wo", m))
            norm("n4", "norm_ffn", KD)
            dve.wait_ge(s_done, 32 + 64)
            moe(1)
            norm("n5", "ple_g", KD)
            embed(1)
            norm("n6", "norm_final", 0)

        @block.scalar
        def _(act):
            act.dma_start(hT[:], a["xT"]).then_inc(s_x, 16)
            act.dma_start(cst[:], a["constants"]).then_inc(s_cst, 16)
            act.dma_start(vt[:], a["vectors"]).then_inc(s_vec, 16)
            act.dma_start(wdw[:], a["tapsT"]).then_inc(s_dw, 16)
            act.dma_start(stT[:, :, :, 0:CW - 1], a["stateT"]).then_inc(s_st, 16)
            act.dma_start(pT[:], a["pT"]).then_inc(s_p, 16)
            act.dma_start(wr[:], a["w_router"]).then_inc(s_wr, 16)
            act.dma_start(br[:], a["b_router"]).then_inc(s_wr, 16)

            def squares(name, src, n, ready, at=0):
                for k in range(n):
                    ready(k)
                    s.activation(sq[:, at + k, :], src[:, k, :], ACT.Square).then_inc(s_sq, 1)

            def root(key):
                freed(act, key)
                s.activation(rstd[:], rstd[:], ACT.Sqrt).then_inc(s_rs, 1)

            def h_ready(key):
                return lambda k: freed(act, key + (k,))

            squares("n0", hT, KD, lambda k: act.wait_ge(s_x, 16))
            root("n0")
            act.wait_ge(s_vec, 16)
            for c in range(KD):
                key = ("pw1", 1, c)
                ps = arrive(act, key)
                if c >= 2:
                    freed(act, ("pw1", 0, c - 2))
                s.activation(sgu[:, c % 2, :], ps[:, 0:T], ACT.Sigmoid, bias=vcol("conv_b_pw1", KD + c))\
                 .then_inc(is_free(key), 1)
            squares("ln", zT, KD, lambda k: act.wait_ge(s_zc, k + 1))
            root("lnv")
            for k in range(KD):
                act.wait_ge(s_zn, k + 1)
                s.activation(xnT[:, k, :], zT[:, k, :], ACT.Silu, bias=vcol("conv_ln_b", k),
                             scale=vcol("conv_ln_g", k)).then_inc(s_zs, 1)
            squares("n1", hT, KD, h_ready(("pw2",)))
            root("n1")

            def moe(l):
                ex = rt["ex"]
                for i, (t0, n) in enumerate(TILES):
                    for hf in range(2):
                        key = ("row", l, i, hf)
                        ps = arrive(act, key)
                        s.copy(XR[0:n, i, hf * 512:(hf + 1) * 512], ps[0:n, :]).then_inc(is_free(key), 1)
                act.wait_ge(s_pre, l + 1)
                s.activation(ex[:], ex[:], ACT.Exp).then_inc(s_ex, 1)
                for hf in range(2):
                    for k in range(0, KD, 2):
                        key = ("xg", l, hf, k)
                        ps = arrive(act, key)
                        s.copy(XGT[:, k, hf * HALF:(hf + 1) * HALF], ps[:, 0:HALF]).then_inc(is_free(key), 1)
                act.wait_ge(s_off, l + 1)
                eb = E * l

                def window_out(it, j):
                    e = 3 * it + j
                    at = act.value_load(offI[0:1, bass.ds(e, 1)], min_val=0, max_val=NPAIR)
                    act.wait_ge(s_dn, e + (eb + 1))
                    if not isinstance(e, int) or e + eb:
                        act.wait_ge(s_out, e + eb)
                    s.copy(OutT[:, :, bass.ds(at, W)], bank[3 + j][:, :].rearrange("p (m w) -> p m w", m=KD))\
                     .then_inc(s_out, 1)

                def body(it, j):
                    e = 3 * it + j
                    act.wait_ge(s_gu, e + (eb + 1))
                    if not isinstance(e, int) or e >= 3:
                        act.wait_ge(s_hid, e + (eb - 2))
                    s.activation(sg[:, j, :, :], bank[j][:, 0:FK * W].rearrange("p (m w) -> p m w", m=FK), ACT.Silu)\
                     .then_inc(s_sg, 1)
                    if j == 0:
                        if not isinstance(it, int) or it:
                            window_out(it - 1, 2)
                    else:
                        window_out(it, j - 1)

                experts(act, body)
                window_out(E // 3, E % 3 - 1)
                act.wait_ge(s_out, eb + E)
                with act.If(act.value_load(mostI[0:1, 0:1], min_val=0, max_val=NPAIR) > W):
                    act.wait_ge(s_hid, eb + E)
                    s.copy(tiny[0:1, 0:1], cst[0:1, 0:1]).then_inc(x_out[l], 1)
                    with act.Fori(0, E) as e:
                        for q in range(NXW):
                            at = act.value_load(xstI[0:1, q, bass.ds(e, 1)], min_val=0, max_val=NPAIR)
                            act.wait_ge(x_gu[l], NXW * e + (q + 1))
                            s.activation(sg[:, 0, :, :], bank[0][:, 0:FK * W].rearrange("p (m w) -> p m w", m=FK),
                                         ACT.Silu).then_inc(x_sg[l], 1)
                            act.wait_ge(x_dn[l], NXW * e + (q + 1))
                            act.wait_ge(x_out[l], NXW * e + (q + 1))
                            s.copy(OutT[:, :, bass.ds(at, W)], bank[3][:, :].rearrange("p (m w) -> p m w", m=KD))\
                             .then_inc(x_out[l], 1)
                    act.wait_ge(x_out[l], NXW * E + 1)
                s.copy(tiny[0:1, 1:2], cst[0:1, 0:1]).then_inc(s_mo, 1)
                for i in range(NST):
                    n = min(P, NPAIR - i * P)
                    key = ("or", l, i, 0)
                    ps = arrive(act, key)
                    s.copy(OutR[0:n, i, 0:512], ps[0:n, :]).then_inc(is_free(key), 1)
                squares("n2" if l == 0 else "n5", hT, KD, h_ready(("mo", l)))
                root("n2" if l == 0 else "n5")

            def embed(l):
                for m in range(KD):
                    key = ("pg", l, m)
                    ps = arrive(act, key)
                    if m >= 2:
                        freed(act, ("pin", l, m - 2))
                    s.activation(sgp[:, m % 2, :], ps[:, 0:T], ACT.Sigmoid).then_inc(is_free(key), 1)

            act.wait_ge(s_done, 32)
            moe(0)
            embed(0)
            squares("n3", hT, KD, lambda k: act.wait_ge(s_ple, k + 1))
            root("n3")
            ps = arrive(act, "kpe")
            squares("q", cqr, KQ, lambda k: freed(act, ("cq", k)))
            squares("kv", kvr, KK, lambda k: freed(act, ("kv", k)), at=KQ)
            root("q")
            root("kv")
            s.copy(kr, ps[:, 0:T]).then_inc(is_free("kpe"), 1)
            for c in range(4):
                ps = arrive(act, ("qp", c))
                s.copy(qpr[:, c, :], ps[:, 0:T]).then_inc(is_free(("qp", c)), 1)
            for m in range(KD):
                ps = arrive(act, ("qn", m))
                s.copy(qnT[:, m, :], ps[:, 0:T]).then_inc(is_free(("qn", m)), 1)
            for i in range(2):
                for hf in range(2):
                    ps = arrive(act, ("V", i, hf))
                    s.copy(V[:, i, hf * 512:(hf + 1) * 512], ps[:, :]).then_inc(is_free(("V", i, hf)), 1)
            ps = arrive(act, "ckr")
            s.copy(ckR[0:TS, :], ps[0:TS, 0:KL]).then_inc(is_free("ckr"), 1)

            nmx = stat[:, 0:2 * H]
            esum = stat[:, 2 * H:4 * H]

            def head_exp(h):
                act.wait_ge(s_ng, h + 1)
                if h >= 2:
                    arrive(act, ("pt", h - 2))
                s.activation(pr[:, h % 2, 0:P], sS[:, h % 2, 0:P], ACT.Exp, bias=nmx[:, 2 * h:2 * h + 1],
                             accum_out=esum[:, 2 * h:2 * h + 1])
                s.activation(pr[:, h % 2, P:384], sS[:, h % 2, P:384], ACT.Exp, bias=nmx[:, 2 * h + 1:2 * h + 2],
                             accum_out=esum[:, 2 * h + 1:2 * h + 2]).then_inc(s_pe, 1)

            def head_weights(h):
                ps = arrive(act, ("pt", h))
                if h >= 4:
                    arrive(act, ("o", (h - 4) // 2))
                s.copy(PT[:, h % 4, :], ps[:, 0:384]).then_inc(is_free(("pt", h)), 1)

            for i in range(H + 1):
                if i < H:
                    head_exp(i)
                if i >= 1:
                    head_weights(i - 1)
            arrive(act, ("o", KD - 1))
            freed(act, "ckr")
            act.dma_start(CN[0:1, :, :], ckR[0:TS, :]).then_inc(s_cn, 16)

            for b in range(TS):
                if b:
                    act.wait_ge(t_pe, b)
                for q2 in range(3):
                    key = ("ss", b, q2)
                    ps = arrive(act, key)
                    n = 512 if q2 < 2 else 1
                    s.mul(sc[0:H, q2 * 512:q2 * 512 + n], ps[0:H, 0:n], SCALE).then_inc(is_free(key), 1)
                act.wait_ge(t_ng, b + 1)
                if b:
                    arrive(act, ("sp", b - 1))
                s.activation(pp[0:H, :], sc[0:H, :], ACT.Exp, bias=sstat[0:H, b:b + 1],
                             accum_out=sstat[0:H, 8 + b:9 + b]).then_inc(t_pe, 1)
            squares("n4", hT, KD, h_ready(("wo",)))
            root("n4")
            act.wait_ge(s_done, 32 + 64)
            moe(1)
            embed(1)
            squares("n6", hT, KD, lambda k: act.wait_ge(s_ple, KD + k + 1))
            root("n6")

        def expert_weights(l, e, c):
            w = a[("moe_w_gate", "moe_w_up", "moe_w_down")[c]][l][bass.ds(e, 1)]
            if c < 2:
                return w.rearrange("o (p k) f -> p (o k f)", k=KD)
            return w.rearrange("o (k p) f -> p (o k) f", k=FK)

        @block.gpsimd
        def _(pool):
            g = nc.gpsimd
            pool.dma_start(pages[:], a["page_table"]).then_inc(s_pg, 16)
            g.memset(uT[:, :, 0:CW - 1], 0.0).then_inc(s_zero, 1)
            g.memset(rt["L"][:], 0.0).then_inc(s_zero, 1)
            g.memset(rt["pos"][:], 0.0).then_inc(s_zero, 1)
            g.memset(rt["gl8"][:], -BIG).then_inc(s_zero, 1)

            freed(pool, ("pw1", 0, KD - 1))
            pool.dma_start(out["csp"], uT[:, :, TP:TP + CW - 1]).then_inc(s_done, 16)
            pool.dma_start(out["css"], stT[:, :, :, 1:CW]).then_inc(s_done, 16)
            made = [0]

            def step(ins):
                made[0] += 1
                ins.then_inc(s_pl, 1)
                pool.wait_ge(s_pl, made[0])

            def moe(l):
                arrive(pool, ("router", l))
                pool.wait_ge(s_done, 32 + 64 * l)
                g.memset(XGT[:, :, NPAIR:XCOLS], 0.0).then_inc(s_pad, 1)
                pool.wait_ge(s_w, l + 1)
                tmp = Gm.rearrange("p a b -> p (a b)")[:, 0:NPAIR]
                for i, (t0, n) in enumerate(TILES):
                    iota = cst[0:n, C_IOTA:C_IOTA + NPAIR]
                    step(g.tensor_scalar(SG[0:n, i, :], iota, rt["slot1"][0:n, i, :], rt["w1"][0:n, i, :],
                                         ALU.is_equal, ALU.mult))
                    step(g.tensor_scalar(tmp[0:n, :], iota, rt["slot2"][0:n, i, :], rt["w2"][0:n, i, :],
                                         ALU.is_equal, ALU.mult))
                    g.tensor_tensor(SG[0:n, i, :], SG[0:n, i, :], tmp[0:n, :], ALU.add).then_inc(s_SG, 1)
                    pool.wait_ge(s_SG, 3 * l + i + 1)
                pool.wait_ge(s_off, l + 1)
                with pool.If(pool.value_load(mostI[0:1, 0:1], min_val=0, max_val=NPAIR) > W):
                    with pool.Fori(0, E) as e:
                        pool.wait_ge(x_out[l], NXW * e + 1)
                        for c, name in enumerate(("moe_w_gate", "moe_w_up", "moe_w_down")):
                            pool.dma_start(exw[:, c, :] if c < 2 else exw[:, c, :].rearrange("p (k f) -> p k f", k=FK),
                                           expert_weights(l, e, c)).then_inc(x_w[l], 16)

            def load_cache(b):
                if b >= 2:
                    arrive(pool, ("sv", b - 2))
                with pool.Fori(0, PAGES) as n:
                    pg = pool.value_load(pages[0:1, bass.ds(n + b * PAGES, 1)], min_val=0,
                                         max_val=a["cache_ckv"].shape[0] - 1)
                    for name, dst in (("cache_ckv", CK[:, b % 2, bass.ds(n * KL, KL)]),
                                      ("cache_ckvT", CKT[b % 2][:, bass.ds(n, 1), :, :]
                                       .rearrange("p g k t -> p (g k t)")),
                                      ("cache_kpeT", KPT[0:DR, b % 2, bass.ds(n * PAGE, PAGE)])):
                        pool.dma_start(dst, a[name][bass.ds(pg, 1)].rearrange("o p f -> p (o f)"))\
                            .then_inc(s_ckin[b % 2], 16)

            moe(0)
            arrive(pool, ("mo", 0, KD - 1))
            pool.wait_ge(s_pg, 16)
            pool.dma_start(wukT, a["ukT"]).then_inc(s_uk, 16)
            arrive(pool, "kpe")
            arrive(pool, "kv")
            load_cache(0)
            load_cache(1)
            pool.wait_ge(s_ck, KK)
            pool.dma_start(out["ckv_p"], ckvT[:, :, 0:TP]).then_inc(s_done, 16)
            pool.dma_start(out["ckv_s"], ckvT[:, :, TP:T]).then_inc(s_done, 16)
            pool.wait_ge(s_kpe, 1)
            pool.dma_start(out["kpe_p"], kpeT[0:DR, 0:TP]).then_inc(s_done, 16)
            pool.dma_start(out["kpe_s"], kpeT[0:DR, TP:T]).then_inc(s_done, 16)
            for b in range(2, TS):
                load_cache(b)
            moe(1)

        @block.sync
        def _(sp):
            last = {}
            for c in range(KD):
                last[G_PW1 + c] = ("pw1", c % 2, 2 * (c // 2) + 1)
            for i in range(4):
                last[G_PW2 + i] = ("pw2", 2 * i + 1)
                last[G_WO + i] = ("wo", 2 * i + 1)
                for l in range(2):
                    last[G_PLE[l] + 1 + i] = ("pg", l, 2 * i + 1)
            for l in range(2):
                last[G_PLE[l]] = ("pin", l, KD - 1)
            for i in range(2):
                last[G_DQ + i] = ("cq", KQ - 1)
                last[G_DKV + i] = "kpe"
            for k in range(KQ):
                last[G_UQ + k] = ("qn", KD - 1)
            last[G_UK] = ("kn", KD - 1)
            last[G_UV] = "so"

            def used_up(g):
                g -= NSLOT
                if g < 0:
                    return
                if g in last:
                    b, u = taken[last[g]]
                    sp.wait_ge(full[b], u + 1)
                else:
                    l = int(g >= G_MOE1)
                    e, c = divmod(g - G_MOE[l], 3)
                    sp.wait_ge(s_gu if c < 2 else s_dn, E * l + e + 1)

            def fill(g):
                used_up(g)
                at = g - (3 * E if g > G_MOE0 else 0) - (3 * E if g > G_MOE1 else 0)
                sp.dma_start(slot(g), a["stream"][at]).then_inc(w_in[g % NSLOT], 16)

            def expert(l, it, j):
                e = 3 * it + j
                for c in range(3):
                    g = G_MOE[l] + 3 * j + c
                    if isinstance(it, int):
                        used_up(g + NSLOT * it)
                    else:
                        sp.wait_ge(s_gu if c < 2 else s_dn, e + (E * l - 2))
                    d = slot(g) if c < 2 else slot(g).rearrange("p (k f) -> p k f", k=FK)
                    sp.dma_start(d, expert_weights(l, e, c)).then_inc(w_in[g % NSLOT], 16)

            for g in range(G_MOE0):
                fill(g)
            experts(sp, lambda it, j: expert(0, it, j))
            for g in range(G_PLE0, G_MOE1):
                fill(g)
            experts(sp, lambda it, j: expert(1, it, j))
            for g in range(G_PLE1, NPIECE):
                fill(g)
            sp.wait_ge(s_xn, 7 * KD)
            sp.dma_start(out["y_p"], xnT[:, :, 0:TP]).then_inc(s_y, 16)
            sp.dma_start(out["y_s"], xnT[:, :, TP:T]).then_inc(s_y, 16)
            sp.wait_ge(s_y, 32)
            sp.wait_ge(s_done, 16 * 6)


def packed(x):
    def chunks(w):
        w = w.reshape(-1, P, *w.shape[1:])
        return np.swapaxes(w, 0, 1)

    def piece(w):
        w = chunks(w).reshape(P, -1)
        return np.concatenate([w, np.zeros((P, SLOT - w.shape[1]), w.dtype)], 1)

    b = {}
    b["xT"] = chunks(np.concatenate([x["x_prompt"][0], x["x_sample"][:, 0]], 0).T)
    p = np.concatenate([x["p_prompt"][:, 0], x["p_sample"][:, :, 0]], 1)
    b["pT"] = np.swapaxes(np.stack([chunks(p[l].T) for l in range(2)]), 0, 1)
    b["vectors"] = np.concatenate([x[n].reshape(-1, P) for n, _ in VEC], 0).T
    b["tapsT"] = x["conv_w_dw"].reshape(CW * KD, P).T
    b["stateT"] = chunks(np.transpose(x["state_conv"][0], (2, 0, 1)))
    wr = np.concatenate([x["moe_w_group"], x["moe_w_expert"]], 2)
    b["w_router"] = np.swapaxes(np.stack([chunks(wr[l]) for l in range(2)]), 0, 1)
    br = np.concatenate([x["moe_b_group"], x["moe_b_expert"]], 1)
    b["b_router"] = np.broadcast_to(br[None], (P, 2, G + E))
    b["page_table"] = x["page_table"].reshape(1, -1)
    b["cache_ckv"] = x["cache_ckv"][:, 0]
    ckv = np.swapaxes(b["cache_ckv"], 1, 2).reshape(-1, KK, P, PAGE)
    b["cache_ckvT"] = np.swapaxes(ckv, 1, 2).reshape(-1, P, KK * PAGE)
    b["cache_kpeT"] = np.swapaxes(x["cache_kpe"][:, 0], 1, 2)
    b["ukT"] = chunks(np.transpose(x["mla_w_uk"][0], (1, 2, 0)).reshape(H * DN, KL))
    s = []
    for i in range(4):
        for kind in range(2):
            s.append(x["conv_w_pw1"][0][:, (4 * kind + i) * 256:(4 * kind + i + 1) * 256])
    s += [x["conv_w_pw2"][0][:, i * 256:(i + 1) * 256] for i in range(4)]

    def ple(l):
        return [x["ple_w_in"][l]] + [x["ple_w_gate"][l][:, i * 256:(i + 1) * 256] for i in range(4)]
    s += ple(0)
    s += [x["mla_w_dq"][0][512 * i:512 * (i + 1)] for i in range(2)]
    dkv = x["mla_w_dkv"][0]
    dkv = np.concatenate([dkv[:, 0:KL]] + [dkv[:, KL:]] * (P // DR), 1)
    s += [dkv[512 * i:512 * (i + 1)] for i in range(2)]
    uq = x["mla_w_uq"][0].reshape(QL, H, DN + DR)
    uq = np.concatenate([uq[:, :, 0:DN].reshape(QL, -1), uq[:, :, DN:].reshape(QL, -1)], 1)
    s += [uq[P * k:P * (k + 1)] for k in range(KQ)]
    s += [x["mla_w_uk"][0].reshape(KL, H * DN), x["mla_w_uv"][0].reshape(KL, H * DV)]
    s += [x["mla_w_o"][0][:, i * 256:(i + 1) * 256] for i in range(4)]
    s += ple(1)
    b["stream"] = np.stack([piece(w) for w in s])
    for n in ("moe_w_gate", "moe_w_up", "moe_w_down"):
        b[n] = x[n]
    b["constants"] = constants()
    return {n: np.ascontiguousarray(w) for n, w in b.items()}


_OUTS = {"y_p": (P, KD, TP), "y_s": (P, KD, TS), "csp": (P, KD, CW - 1), "css": (P, KD, TS, CW - 1),
         "ckv_p": (P, KK, TP), "kpe_p": (DR, TP), "ckv_s": (P, KK, TS), "kpe_s": (DR, TS)}


def kernel(**inputs):
    import concourse.bacc as bacc
    from concourse.bass_utils import run_bass_kernel_spmd as run

    nc = bacc.Bacc("TRN2", target_bir_lowering=False, num_devices=1)
    arrays = packed({n: np.asarray(x) for n, x in inputs.items()})
    a = {n: nc.dram_tensor("in_" + n, x.shape, mybir.dt.from_np(x.dtype), kind="ExternalInput").ap()
         for n, x in arrays.items()}
    out = {n: nc.dram_tensor("out_" + n, shape, F32, kind="ExternalOutput").ap() for n, shape in _OUTS.items()}
    build(nc, a, out)
    r = run(nc, [{"in_" + n: x for n, x in arrays.items()}], core_ids=[0]).results[0]

    def rows(name):
        y = np.moveaxis(r["out_" + name], 0, 1)
        return np.moveaxis(y.reshape(-1, *y.shape[2:]), 0, -1)

    return (rows("y_p")[None], rows("y_s")[:, None], rows("csp")[None, None], rows("css")[None],
            rows("ckv_p")[None, None], r["out_kpe_p"].T[None, None], rows("ckv_s")[None, :, None],
            r["out_kpe_s"].T[None, :, None])
```

```python
from contextlib import ExitStack

import numpy as np

import concourse.bass as bass
from concourse import mybir

F32 = mybir.dt.float32
I32 = mybir.dt.int32
U32 = mybir.dt.uint32
ALU = mybir.AluOpType
ACT = mybir.ActivationFunctionType
AX = mybir.AxisListType

P = 128
D = 1024
KD = D // P
TP, TS = 256, 8
T = TP + TS
TILES = [(0, 128), (128, 128), (256, TS)]
EPS = 1e-6
CW = 31
E, G, EG = 32, 4, 8
F = 256
FK = F // P
NPAIR = 2 * T
W = 64
XCOLS = NPAIR + W
NXW = (T + W - 1) // W - 1
XROWS = (NXW + 1) * W
HALF = NPAIR // 2
PLE = 256
H, DN, DR, DV = 16, 64, 32, 64
QL, KL = 384, 256
KQ, KK = QL // P, KL // P
PAGES, PAGE = 8, 128
PAST = PAGES * PAGE
SB = 4
HP = 32
SCALE = float(1.0 / np.sqrt(DN + DR))
NEG = -1e30
BIG = 3e38
SLOT = 2048
NSLOT = 9
ARENA = 21840

C_ID, C_ONE, C_TRI, C_ROT, C_COS, C_SIN = 0, 128, 256, 384, 512, 512 + T
C_MASK = C_SIN + T
C_IOTA = C_MASK + 384
C_GRP = C_IOTA + NPAIR
C_W64 = C_GRP + E
C_BASE = C_W64 + NXW * E
C_NEW = C_BASE + 2 * E
C_BAT = C_NEW + TS
C_ALL = C_BAT + TS // SB

VEC = [("norm_mix", 2 * KD), ("norm_ffn", 2 * KD), ("ple_g", 2 * KD), ("norm_final", KD), ("conv_ln_g", KD),
       ("conv_ln_b", KD), ("conv_b_dw", KD), ("conv_b_pw1", 2 * KD), ("mla_g_q", KQ), ("mla_g_kv", KK)]
VCOL, NVEC = {}, 0
for _name, _n in VEC:
    VCOL[_name] = NVEC
    NVEC += _n

CONV_DVE, CONV_POOL, CONV_PE = [(0, 1, 2), (4, 5)], 3, [6, 7]
Z_ORDER = [0, 1, 2, 4, 5, 3, 6, 7]
GLU_AT = [6, 12, 18, 24, 30]
SAMPLE_AT = [3, 5, 7, 9]

G_PW1, G_PW2, G_MOE0 = 0, 8, 12
G_PLE0 = G_MOE0 + 3 * E
G_DQ = G_PLE0 + 5
G_DKV, G_UQ, G_UK, G_UV, G_WO = G_DQ + 2, G_DQ + 4, G_DQ + 7, G_DQ + 8, G_DQ + 9
G_MOE1 = G_WO + 4
G_PLE1 = G_MOE1 + 3 * E
NPIECE = G_PLE1 + 5
G_MOE, G_PLE = [G_MOE0, G_MOE1], [G_PLE0, G_PLE1]

NORMS = []
SQ = {}
_n = 0
for _name, _c in [("n0", 8), ("ln", 8), ("n1", 8), ("n2", 8), ("n3", 8), ("q", KQ), ("kv", KK), ("n4", 8), ("n5", 8),
                  ("n6", 8)]:
    NORMS.append(_name if _name != 'ln' else 'lnv')
    SQ[_name] = _n
    _n += _c


def constants():
    c = np.zeros((P, C_ALL), np.float32)
    i = np.arange(P)
    c[:, C_ID:C_ID + P] = np.eye(P)
    c[:, C_ONE:C_ONE + P] = 1
    c[:, C_TRI:C_TRI + P] = i[:, None] < i[None, :]
    for m in range(P):
        if m % DR < DR // 2:
            c[m + DR // 2, C_ROT + m] = -1
        else:
            c[m - DR // 2, C_ROT + m] = 1
    pos = np.concatenate([np.arange(TP), np.full(TS, PAST)]).astype(np.float32)
    freq = np.power(np.float32(10000.0), -np.arange(DR // 2, dtype=np.float32) / np.float32(DR // 2))
    ang = (pos[None, :] * freq[i % (DR // 2)][:, None]).astype(np.float32)
    c[:, C_COS:C_COS + T] = np.cos(ang)
    c[:, C_SIN:C_SIN + T] = np.sin(ang)
    later = np.where(i[None, :] > i[:, None], NEG, 0)
    c[:, C_MASK:C_MASK + P] = later
    c[:, C_MASK + 2 * P:C_MASK + 3 * P] = later
    c[:, C_IOTA:C_IOTA + NPAIR] = np.arange(NPAIR)
    c[:, C_GRP:C_GRP + E] = np.arange(E) // EG
    c[:, C_W64:C_BASE] = np.repeat(W * np.arange(1, NXW + 1), E)
    c[:, C_NEW:C_BAT] = np.arange(TS) % SB == i[:, None] // HP
    c[:, C_BAT:] = np.arange(TS // SB) == i[:, None] // SB
    c[:, C_BASE:C_NEW] = np.concatenate([W * np.arange(E), XROWS * np.arange(E)])
    return c


def build(nc, a, out, erows, xrows):
    NPOOL = a["cache_ckv"].shape[0]

    with ExitStack() as ctx:
        def sb(name, shape, dt=F32):
            return ctx.enter_context(nc.sbuf_tensor(name, shape, dt))

        def sem(name):
            return ctx.enter_context(nc.semaphore(name))

        ring = sb("ring", [P, NSLOT, SLOT])
        cst = sb("cst", [P, C_ALL])
        hT = sb("hT", [P, KD, T])
        xn_sq = sb("xn_sq", [P, 2, KD, T])
        xnT, sq = xn_sq[:, 0], xn_sq[:, 1]
        pT = sb("pT", [P, 2, 2, T])
        vt = sb("vt", [P, NVEC])
        wdw = sb("wdw", [P, CW * KD])
        wr = sb("wr", [P, 2, KD, G + E])
        br = sb("br", [P, 2, G + E])
        rstd = sb("rstd", [P, T])
        pages = sb("pages", [1, TS * PAGES], I32)
        arena = sb("arena", [P, ARENA])
        bank = [ctx.enter_context(nc.psum_tensor(f"bank{i}", [P, 512], F32)) for i in range(8)]

        def place(at, *shape):
            n = int(np.prod(shape))
            v = arena[:, at:at + n]
            if len(shape) == 2:
                v = v.rearrange("p (a b) -> p a b", a=shape[0])
            elif len(shape) == 3:
                v = v.rearrange("p (a b c) -> p a b c", a=shape[0], b=shape[1])
            return v, at + n

        uT, q = place(0, KD, CW - 1 + TP)
        zT, q = place(q, KD, T)
        stT, q = place(q, KD, TS, CW)
        sgu, q = place(q, 4, T)
        ctmp, q = place(q, TS, CW)
        mu, q = place(q, T)
        dg, q = place(q, len(CONV_PE), CW, P)
        tapped, q = place(q, 2, TP)
        XR, q = place(0, 3, D)
        S, q = place(q, 3, NPAIR)
        exw, _ = place(0, 3, SLOT)
        R, _ = place(0, 3, 2, D)
        XGT, q = place(3 * SLOT, KD, XCOLS)
        q_xe = q
        xe, q = place(q, 3, KD, W)
        sg, q = place(q, 3, P)
        hid, q = place(q, 3, P)
        hidT, q = place(q, 3, FK * 64)
        orow, q = place(q, 3, D // 2)
        pinT, q = place(q, KD, T)
        rt = {}
        for name, n in (("L", G + E), ("gl8", 8), ("gmx", 8), ("em", E), ("G32", E), ("emx", 8), ("M1", E), ("M2", E),
                        ("M", E), ("pos", E), ("ex", 5), ("eidx", 2), ("gidx", 1), ("gsum", 1), ("den", 1), ("ridx", 2), ("w1", 1),
                        ("w2", 1), ("slot1", 1), ("slot2", 1)):
            rt[name] = sb("rt_" + name, [P, 3, n])
        gix = sb("gix", [P, 3, 8], U32)
        eix = sb("eix", [P, 3, 8], U32)
        cnt = sb("cnt", [P, E])
        incl = sb("incl", [P, E])
        off = sb("off", [P, E])
        most = sb("most", [P, 1])
        offI = sb("offI", [P, E], I32)
        mostI = sb("mostI", [P, 1], I32)
        xst = sb("xst", [P, NXW, E])
        xstI = sb("xstI", [P, NXW, E], I32)
        idx = [sb(f"idx{i}", [P, 3, 2], U32) for i in range(2)]
        sgp, q = place(q_xe, 2, T)
        tgp, q = place(q, 2, T)
        qnT, q = place(0, KD, T)
        qpeT, q = place(q, 4, T)
        oT, q = place(q, KD, T)
        wukT = oT.rearrange("p a b -> p (a b)")[:, 0:KD * KL].rearrange("p (a b) -> p a b", a=KD)
        ckvT, q = place(q, KK, T)
        kpeT, q = place(q, T)
        ckR, q = place(q, KL)
        qlat, q = place(q, KK, TS, HP)
        olat, q = place(q, KK, H, TS)
        qps, q = place(q, TS, HP)
        b0 = q
        knT, q = place(b0, KD, TP)
        V, q = place(q, 2, H * DV)
        b1 = q
        sS, q = place(q, 2, 384)
        pr, q = place(q, 3, 384)
        PT, q = place(q, 3, 384)
        b2 = q
        page0, q = place(q, PAGES, 2 * KL)
        KPT, q = place(q, PAST)
        PTs, q = place(q, PAGES, P)
        qpr, q3 = place(q, 4, T)
        pp, q2 = place(q, PAST + 1)
        pnew, q2 = place(q2, TS)
        assert q2 <= q3
        q = q3
        PTn = wdw[0:TS, 0:P]
        orows = rstd[:, 0:KL]
        cqr, q2 = place(b1, KQ, T)
        kvr, q2 = place(q2, KK, T)
        kr, q2 = place(q2, T)
        rtmp, q2 = place(q2, 2, T)
        cqT, q2 = place(q2, KQ, T)
        assert q2 <= b2
        stat, q = place(q, 6 * H)
        sstat, q = place(q, 2, 8)
        spent, q = place(q, 2)
        assert q <= ARENA, q
        page1 = xn_sq[:].rearrange("p a b c -> p (a b c)")[:, 0:PAGES * 2 * KL].rearrange("p (g f) -> p g f", g=PAGES)
        CKX = [page0, page1] + [ring[:, i:i + 2, :].rearrange("p a b -> p (a b)").rearrange("p (g f) -> p g f", g=PAGES)
                                for i in (G_UQ % NSLOT, G_UQ % NSLOT + 2)]
        CKT = [x[:, :, KL:2 * KL].rearrange("p g (k t) -> p g k t", k=KK) for x in CKX]

        ident = cst[:, C_ID:C_ID + P]
        ones = cst[:, C_ONE:C_ONE + P]
        tri = cst[:, C_TRI:C_TRI + P]

        full = [sem(f"bank_full{i}") for i in range(8)]
        free = [sem(f"bank_free{i}") for i in range(8)]
        w_in = [sem(f"w_in{i}") for i in range(NSLOT)]
        s_cst, s_x, s_vec, s_dw, s_st, s_p, s_wr, s_pg = (sem("in_" + n) for n in
                                                         ("cst", "x", "vec", "dw", "st", "p", "wr", "pages"))
        s_uk = sem("in_ukT")
        s_sq = sem("squares")
        s_xn = sem("xn_chunks")
        s_rs = sem("roots")
        s_dve = sem("dve_steps")
        s_act = sem("act_steps")
        s_pl = sem("pool_steps")
        s_cv = sem("conv_steps")
        s_z = sem("conv_chunks")
        s_zc = sem("centred_chunks")
        s_zn = sem("normed_chunks")
        s_zs = sem("silu_chunks")
        s_zero = sem("pads_zeroed")
        s_dg = sem("tap_diagonals")
        s_zm = sem("pool_products")
        s_zp = sem("pool_taps")
        s_pad = sem("window_pad_zeroed")
        s_ex = sem("router_exp")
        s_pre = sem("router_diffs")
        s_hot = sem("pair_masks")
        s_w = sem("pair_gates")
        s_slot = sem("pair_slots")
        s_S = sem("selection")
        s_off = sem("offsets")
        s_idx = sem("row_indices")
        s_xe = sem("window_in")
        s_gu = sem("gate_up_done")
        s_sg = sem("silu_done")
        s_hid = sem("hidden_done")
        s_tr = sem("hidden_turned")
        s_ht = sem("hidden_T_in")
        s_dn = sem("down_done")
        s_out = sem("window_out")
        s_row = [sem(f"rows_stored{i}") for i in range(3)]
        s_gat = [sem(f"rows_gathered{i}") for i in range(3)]
        x_copy = [sem(f"x{i}_copied") for i in range(2)]
        s_g1 = sem("first_gated")
        s_mix = sem("pairs_added")
        s_ple = sem("h_embedded")
        s_gb = sem("gates_done")
        x_w, x_xe, x_gu, x_sg, x_hid, x_tr, x_ht, x_dn, x_out, x_row = (
            [sem(f"x{i}_{n}") for i in range(2)] for n in
            ("w", "in", "gu", "silu", "hid", "tr", "ht", "down", "out", "row"))
        s_cq, s_ck, s_kpe, s_qp = (sem("mla_" + n) for n in ("cq", "ckv", "kpe", "qpe"))
        s_qps = sem("mla_qpe_samples")
        s_ng, s_pe, s_pn = (sem("att_" + n) for n in ("max", "exp", "p"))
        s_ckin = [sem(f"cache{i}") for i in range(SB)]
        s_kpin = sem("cache_kpe")
        s_qz = sem("queries_padded")
        t_ng, t_pe, t_pn, t_tt, t_or, t_rs = (sem("sam_" + n) for n in
                                              ("max", "exp", "new_p", "p_turned", "rows", "sum_inverse"))
        s_done = sem("stores")
        s_y = sem("y_stored")

        taken, used, turn = {}, [0] * 8, [0]

        def open_bank(pe, key):
            b = turn[0] % 8
            turn[0] += 1
            taken[key] = (b, used[b])
            if used[b]:
                pe.wait_ge(free[b], used[b])
            used[b] += 1
            return bank[b]

        def is_full(key):
            return full[taken[key][0]]

        def arrive(eng, key):
            b, u = taken[key]
            eng.wait_ge(full[b], u + 1)
            return bank[b]

        def is_free(key):
            return free[taken[key][0]]

        def freed(eng, key):
            b, u = taken[key]
            eng.wait_ge(free[b], u + 1)

        def slot(g):
            return ring[:, g % NSLOT, :]

        def landed(eng, g):
            eng.wait_ge(w_in[g % NSLOT], 16 * (g // NSLOT + 1))

        def experts(eng, body):
            for j in range(3):
                body(0, j)
            with eng.Fori(1, E // 3) as it:
                for j in range(3):
                    body(it, j)
            for j in range(E % 3):
                body(E // 3, j)

        def gu_slots(l, j):
            g = (G_MOE[l] + 3 * j) % NSLOT
            return ring[:, g:g + 2, :]

        def stored(layers, j):
            return 32 * layers * len(range(j, E, 3))

        erow = erows.rearrange("(e w) (c d) -> e w c d", e=E, c=2)
        xrow = xrows.rearrange("(e x w) (c d) -> e x w c d", e=E, x=NXW + 1, c=2)

        def piece_turn(l, it, j, c):
            return 16 * it + 16 * ((G_MOE[l] + 3 * j + c) // NSLOT + 1)

        block = ctx.enter_context(nc.Block())
        mm = nc.tensor.matmul
        tr = nc.tensor.transpose

        @block.tensor
        def _(pe):
            pe.wait_ge(s_cst, 16)

            def sum_squares(key, src, n, base):
                ps = open_bank(pe, key)
                for k in range(n):
                    pe.wait_ge(s_sq, base + k + 1)
                    t = mm(ps[:, 0:T], ones, src[:, k, :], start=(k == 0), stop=(k == n - 1))
                t.then_inc(is_full(key), 1)

            def chunk(key, n, lhs, rhs, cols=T, wait=None):
                ps = open_bank(pe, key)
                for k in range(n):
                    if wait:
                        wait(k)
                    t = mm(ps[:, 0:cols], lhs(k), rhs(k), start=(k == 0), stop=(k == n - 1))
                t.then_inc(is_full(key), 1)

            sum_squares("n0", sq, KD, SQ["n0"])
            for c in range(KD):
                for kind in range(2):
                    g = G_PW1 + 2 * (c // 2) + kind
                    w = slot(g).rearrange("p (k f) -> p k f", k=KD)
                    landed(pe, g)

                    def wait(k):
                        if c == 0 and kind == 0:
                            pe.wait_ge(s_xn, k + 1)
                    chunk(("pw1", kind, c), KD, lambda k: w[:, k, (c % 2) * P:(c % 2 + 1) * P],
                          lambda k: xnT[:, k, :], wait=wait)
            for i, c in enumerate(CONV_PE):
                freed(pe, ("pw1", 0, c))
                chunk(("taps", c), CW, lambda j: dg[:, i, j, :], lambda j: uT[:, c, j:j + TP], cols=TP,
                      wait=lambda j: pe.wait_ge(s_dg, CW * i + j + 1))
            chunk("lnm", KD, lambda k: ones, lambda k: zT[:, Z_ORDER[k], :], wait=lambda k: pe.wait_ge(s_z, k + 1))
            sum_squares("lnv", sq, KD, SQ["ln"])
            for m in range(KD):
                g = G_PW2 + m // 2
                w = slot(g).rearrange("p (k f) -> p k f", k=KD)
                landed(pe, g)
                chunk(("pw2", m), KD, lambda k: w[:, k, (m % 2) * P:(m % 2 + 1) * P], lambda k: xnT[:, k, :],
                      wait=(lambda k: pe.wait_ge(s_zs, k + 1)) if m == 0 else None)
            sum_squares("n1", sq, KD, SQ["n1"])

            def moe(l, norm):
                ps = open_bank(pe, ("router", l))
                pe.wait_ge(s_wr, 32)
                for i, (t0, n) in enumerate(TILES):
                    for k in range(KD):
                        if i == 0:
                            pe.wait_ge(s_xn, KD * norm + k + 1)
                        t = mm(ps[0:n, i * (G + E):(i + 1) * (G + E)], xnT[:, k, t0:t0 + n], wr[:, l, k, :],
                               start=(k == 0), stop=(k == KD - 1))
                t.then_inc(is_full(("router", l)), 1)
                for i, (t0, n) in enumerate(TILES):
                    for hf in range(2):
                        ps = open_bank(pe, ("row", l, i, hf))
                        for k in range(4):
                            t = tr(ps[0:n, k * P:(k + 1) * P], xnT[:, 4 * hf + k, t0:t0 + n], ident)
                        t.then_inc(is_full(("row", l, i, hf)), 1)
                ps = open_bank(pe, ("rank", l))
                pe.wait_ge(s_hot, l + 1)
                M = rt["M"]
                for i, (t0, n) in enumerate(TILES):
                    for b in range(i + 1):
                        m = TILES[b][1]
                        mm(ps[0:n, i * E:(i + 1) * E], (tri if b == i else ones)[0:m, 0:n], M[0:m, b, :],
                           start=(b == 0), stop=(b == i))
                for b in range(3):
                    m = TILES[b][1]
                    t = mm(ps[:, 3 * E:4 * E], ones[0:m, :], M[0:m, b, :], start=(b == 0), stop=(b == 2))
                t.then_inc(is_full(("rank", l)), 1)
                for i in range(3):
                    for hf in range(2):
                        freed(pe, ("row", l, i, hf))
                for hf in range(2):
                    for k in range(KD):
                        ps = open_bank(pe, ("xg", l, hf, k))
                        for i, (t0, n) in enumerate(TILES):
                            if hf == 0 and k == 0:
                                pe.wait_ge(s_S, 3 * l + i + 1)
                            t = mm(ps[:, 0:HALF], XR[0:n, i, k:D:KD], S[0:n, i, hf * HALF:(hf + 1) * HALF],
                                   start=(i == 0), stop=(i == 2))
                        t.then_inc(is_full(("xg", l, hf, k)), 1)
                for b in range(7):
                    if used[b]:
                        pe.wait_ge(free[b], used[b])
                eb = E * l

                def gate_up(b, x, w, ks):
                    for k in ks:
                        for c in range(2):
                            t = mm(b[64 * c:64 * c + W, 0:F].rearrange("p (c f) -> p c f", c=2), x[:, k, :],
                                   w[:, :, k * F + c * P:k * F + (c + 1) * P], start=(k == 0), stop=(k == KD - 1))
                    return t

                def turn(rows):
                    for c in range(2):
                        t = mm(bank[3][64 * c:64 * c + 64, 0:P], rows[:, 64 * c:64 * c + 64], ident, start=True,
                               stop=True)
                    return t

                def down(b, x, w):
                    w = w.rearrange("p (k f) -> p k f", k=FK)
                    for k in range(FK):
                        for c in range(2):
                            t = mm(b[64 * c:64 * c + W, :], x[:, 64 * k:64 * k + W], w[:, k, c * 512:(c + 1) * 512],
                                   start=(k == 0), stop=(k == FK - 1))
                    return t

                def first_half(it, j):
                    e = 3 * it + j
                    pe.wait_ge(s_xe, e + (eb + 1))
                    if not isinstance(e, int) or e >= 3:
                        pe.wait_ge(s_hid, e + (eb - 2))
                    for c in range(2):
                        pe.wait_ge(w_in[(G_MOE[l] + 3 * j + c) % NSLOT], piece_turn(l, it, j, c))
                    gate_up(bank[j], xe[:, j, :, :], gu_slots(l, j), range(KD // 2))

                def second_half(it, j):
                    gate_up(bank[j], xe[:, j, :, :], gu_slots(l, j), range(KD // 2, KD)).then_inc(s_gu, 1)

                def body(it, j):
                    e = 3 * it + j
                    more = not isinstance(e, int) or e + 1 < E
                    ahead = (it, j + 1) if j < 2 else (it + 1, 0)
                    if more:
                        first_half(*ahead)
                    pe.wait_ge(s_hid, e + (eb + 1))
                    turn(hid[:, j, :]).then_inc(s_tr, 1)
                    if more:
                        second_half(*ahead)
                    pe.wait_ge(s_ht, e + (eb + 1))
                    if not isinstance(e, int) or e >= 3:
                        pe.wait_ge(s_out, e + (eb - 2))
                    pe.wait_ge(w_in[(G_MOE[l] + 3 * j + 2) % NSLOT], piece_turn(l, it, j, 2))
                    down(bank[4 + j], hidT[:, j, :], slot(G_MOE[l] + 3 * j + 2)).then_inc(s_dn, 1)

                first_half(0, 0)
                second_half(0, 0)
                experts(pe, body)
                pe.wait_ge(s_out, eb + E)
                pe.wait_ge(s_p, 16)
                win = slot(G_PLE[l]).rearrange("p (k f) -> p k f", k=2)
                landed(pe, G_PLE[l])
                for m in range(KD):
                    chunk(("pin", l, m), 2, lambda k: win[:, k, m * P:(m + 1) * P], lambda k: pT[:, l, k, :])
                pe.wait_ge(s_off, l + 1)
                with pe.If(pe.value_load(mostI[0:1, 0:1], min_val=0, max_val=NPAIR) > W):
                    for m in range(KD):
                        freed(pe, ("pin", l, m))
                    with pe.Fori(0, E) as e:
                        for i in range(NXW):
                            pe.wait_ge(x_w[l], 48 * e + 48)
                            pe.wait_ge(x_xe[l], NXW * e + (i + 1))
                            gate_up(bank[0], xe[:, 0, :, :], exw[:, 0:2, :], range(KD)).then_inc(x_gu[l], 1)
                            pe.wait_ge(x_hid[l], NXW * e + (i + 1))
                            turn(hid[:, 0, :]).then_inc(x_tr[l], 1)
                            pe.wait_ge(x_ht[l], NXW * e + (i + 1))
                            down(bank[4], hidT[:, 0, :], exw[:, 2, :]).then_inc(x_dn[l], 1)
                ps = [open_bank(pe, ("mo", l, k)) for k in range(KD)]
                for i, (t0, n) in enumerate(TILES):
                    pe.wait_ge(s_mix, 3 * l + i + 1)
                    for k in range(KD):
                        t = tr(ps[k][:, t0:t0 + n], R[0:n, i, 0, k * P:(k + 1) * P], ident[0:n, 0:n])
                        if i == 2:
                            t.then_inc(is_full(("mo", l, k)), 1)

            def embed(l, norm):
                for m in range(KD):
                    g = G_PLE[l] + 1 + m // 2
                    w = slot(g).rearrange("p (k f) -> p k f", k=KD)
                    landed(pe, g)
                    chunk(("pg", l, m), KD, lambda k: w[:, k, (m % 2) * P:(m % 2 + 1) * P], lambda k: xnT[:, k, :],
                          wait=(lambda k: pe.wait_ge(s_xn, KD * norm + k + 1)) if m == 0 else None)

            moe(0, 1)
            sum_squares("n2", sq, KD, SQ["n2"])
            embed(0, 2)
            sum_squares("n3", sq, KD, SQ["n3"])

            def dkv(k):
                return slot(G_DKV + k // 4)[:, 0:4 * (KL + P)].rearrange("p (k f) -> p k f", k=4)[:, k % 4, :]

            def dq(k):
                return slot(G_DQ + k // 4)[:, 0:4 * QL].rearrange("p (k f) -> p k f", k=4)[:, k % 4, :]

            for g in (G_DQ, G_DQ + 1, G_DKV, G_DKV + 1):
                landed(pe, g)
            for m in range(KQ):
                chunk(("cq", m), KD, lambda k: dq(k)[:, m * P:(m + 1) * P], lambda k: xnT[:, k, :],
                      wait=(lambda k: pe.wait_ge(s_xn, KD * 3 + k + 1)) if m == 0 else None)
            for m in range(KK):
                chunk(("kv", m), KD, lambda k: dkv(k)[:, m * P:(m + 1) * P], lambda k: xnT[:, k, :])
            chunk("kpe", KD, lambda k: dkv(k)[:, KL:KL + P], lambda k: xnT[:, k, :])
            sum_squares("q", sq, KQ, SQ["q"])
            sum_squares("kv", sq[:, KQ:KQ + KK, :], KK, SQ["kv"])
            freed(pe, "kpe")
            chunk("krot", 1, lambda k: cst[:, C_ROT:C_ROT + P], lambda k: kr)
            uq = [slot(G_UQ + k) for k in range(KQ)]
            for k in range(KQ):
                landed(pe, G_UQ + k)
            for c in range(4):
                chunk(("qp", c), KQ, lambda k: uq[k][:, H * DN + c * P:H * DN + (c + 1) * P], lambda k: cqT[:, k, :],
                      wait=(lambda k: pe.wait_ge(s_cq, k + 1)) if c == 0 else None)
            for c in range(4):
                for m in (2 * c, 2 * c + 1):
                    chunk(("qn", m), KQ, lambda k: uq[k][:, m * P:(m + 1) * P], lambda k: cqT[:, k, :])
                freed(pe, ("qp", c))
                chunk(("qrot", c), 1, lambda k: cst[:, C_ROT:C_ROT + P], lambda k: qpr[:, c, :])
            landed(pe, G_UK)
            landed(pe, G_UV)
            uk = slot(G_UK).rearrange("p (k f) -> p k f", k=KK)
            uv = slot(G_UV).rearrange("p (k f) -> p k f", k=KK)
            for c in range(KD):
                chunk(("kn", c), KK, lambda k: uk[:, k, c * P:(c + 1) * P], lambda k: ckvT[:, k, 0:TP], cols=TP,
                      wait=(lambda k: pe.wait_ge(s_ck, k + 1)) if c == 0 else None)
            for i in range(2):
                for hf in range(2):
                    chunk(("V", i, hf), KK, lambda k: ckvT[:, k, i * P:(i + 1) * P],
                          lambda k: uv[:, k, hf * 512:(hf + 1) * 512], cols=512)
            ps = open_bank(pe, "ckr")
            for k in range(KK):
                t = tr(ps[0:TS, k * P:(k + 1) * P], ckvT[:, k, TP:T], ident)
            t.then_inc(is_full("ckr"), 1)
            pe.wait_ge(s_uk, 16)
            for m in range(KD):
                freed(pe, ("qn", m))
            for odd in range(2):
                ps = open_bank(pe, ("ql", odd))
                r = slice(DN * odd, DN * odd + DN)
                for c in range(KD):
                    for k in range(KK):
                        t = mm(ps[:, (k * KD + c) * TS:(k * KD + c + 1) * TS], wukT[r, c, k * P:(k + 1) * P],
                               qnT[r, c, TP:T], start=True, stop=True)
                t.then_inc(is_full(("ql", odd)), 1)

            def scores(h):
                ps = open_bank(pe, ("sc", h))
                c, r = h // 2, slice(DN * (h % 2), DN * (h % 2) + DN)
                c4, r4 = h // 4, slice(DR * (h % 4), DR * (h % 4) + DR)
                if h == 0:
                    for m in range(KD):
                        freed(pe, ("kn", m))
                if h % 4 == 0:
                    pe.wait_ge(s_qp, h // 4 + 1)
                for i in range(2):
                    o = ps[:, P * i:P * i + P * (i + 1)]
                    mm(o, qnT[r, c, i * P:(i + 1) * P], knT[r, c, 0:(i + 1) * P], start=True, stop=False)
                    t = mm(o, qpeT[r4, c4, i * P:(i + 1) * P], kpeT[r4, 0:(i + 1) * P], start=False, stop=True)
                t.then_inc(is_full(("sc", h)), 1)

            def turn_weights(h):
                ps = open_bank(pe, ("pt", h))
                pe.wait_ge(s_pn, h + 1)
                for k in range(3):
                    t = tr(ps[:, k * P:(k + 1) * P], pr[:, h % 3, k * P:(k + 1) * P], ident)
                t.then_inc(is_full(("pt", h)), 1)

            def values(h):
                c, r = h // 2, slice(DV * (h % 2), DV * (h % 2) + DV)
                if h % 2 == 0:
                    open_bank(pe, ("o", c))
                ps = bank[taken[("o", c)][0]]
                freed(pe, ("pt", h))
                if h == 0:
                    for i in range(2):
                        for hf in range(2):
                            freed(pe, ("V", i, hf))
                v = [V[:, i, h * DV:(h + 1) * DV] for i in range(2)]
                mm(ps[r, 0:P], v[0], PT[:, h % 3, 0:P], start=True, stop=True)
                mm(ps[r, P:2 * P], v[0], PT[:, h % 3, P:2 * P], start=True, stop=False)
                t = mm(ps[r, P:2 * P], v[1], PT[:, h % 3, 2 * P:3 * P], start=False, stop=True)
                if h % 2:
                    t.then_inc(is_full(("o", c)), 1)

            def sample_scores(B):
                if B == 0:
                    freed(pe, ("ql", 0))
                    freed(pe, ("ql", 1))
                    pe.wait_ge(s_qps, 4 * SB)
                for i in range(SB):
                    pe.wait_ge(s_ckin[i], 16 * PAGES * (B + 1))
                pe.wait_ge(s_kpin, 16 * PAGES * SB * (B + 1))
                for q2 in range(3):
                    ps = open_bank(pe, ("ss", B, q2))
                    n = 512 if q2 < 2 else 1
                    for k in range(KK + 1):
                        for i in range(SB):
                            b = SB * B + i
                            if k < KK:
                                keys = CKT[i][:, 4 * q2:4 * q2 + 4, k, :] if q2 < 2 else ckvT[:, k, TP + b:TP + b + 1]
                            else:
                                keys = KPT[:, q2 * 512:(q2 + 1) * 512] if q2 < 2 else kpeT[:, TP + b:TP + b + 1]
                            t = mm(ps[HP * i:HP * (i + 1), 0:n], qlat[:, k, b, :] if k < KK else qps[:, b, :], keys,
                                   start=(k == 0), stop=(k == KK))
                    t.then_inc(is_full(("ss", B, q2)), 1)

            def sample_weights(B):
                pe.wait_ge(t_pe, B + 1)
                for hf in range(2):
                    ps = open_bank(pe, ("sp", B, hf))
                    for g in range(4):
                        t = tr(ps[:, g * P:(g + 1) * P], pp[:, (4 * hf + g) * P:(4 * hf + g + 1) * P], ident)
                    t.then_inc(is_full(("sp", B, hf)), 1)
                ps = open_bank(pe, ("sn", B))
                pe.wait_ge(t_pn, B + 1)
                tr(ps[0:TS, 0:P], pnew, ident).then_inc(is_full(("sn", B)), 1)

            def sample_values(B):
                for hf in range(2):
                    freed(pe, ("sp", B, hf))
                freed(pe, ("sn", B))
                ps = open_bank(pe, ("sv", B))
                for g in range(PAGES):
                    for i in range(SB):
                        mm(ps[HP * i:HP * (i + 1), 0:KL], PTs[:, g, HP * i:HP * (i + 1)], CKX[i][:, g, 0:KL],
                           start=(g == 0), stop=False)
                mm(ps[:, 0:KL], PTn, ckR[0:TS, :], start=False, stop=True).then_inc(is_full(("sv", B)), 1)

            def sample_out(B):
                pe.wait_ge(t_or, B + 1)
                ps = open_bank(pe, ("st", B))
                for k in range(KK):
                    t = tr(ps[:, k * P:(k + 1) * P], orows[:, k * P:(k + 1) * P], ident)
                t.then_inc(is_full(("st", B)), 1)

            for i in range(H + 3):
                if i < H:
                    scores(i)
                if 2 <= i < H + 2:
                    turn_weights(i - 2)
                if i >= 3:
                    values(i - 3)
                if i in SAMPLE_AT:
                    (sample_scores, sample_weights, sample_values, sample_out)[SAMPLE_AT.index(i)](0)
            sample_scores(1)
            sample_weights(1)
            sample_values(1)
            sample_out(1)
            ps = open_bank(pe, "so")
            for B in range(TS // SB):
                freed(pe, ("st", B))
            for h in range(H):
                c, r = h // 2, slice(DV * (h % 2), DV * (h % 2) + DV)
                for k in range(KK):
                    t = mm(ps[r, c * TS:(c + 1) * TS], uv[:, k, h * DV:(h + 1) * DV], olat[:, k, h, :],
                           start=(k == 0), stop=(k == KK - 1))
            t.then_inc(is_full("so"), 1)
            freed(pe, "so")
            for c in range(KD):
                freed(pe, ("o", c))
            for m in range(KD):
                g = G_WO + m // 2
                w = slot(g).rearrange("p (k f) -> p k f", k=KD)
                landed(pe, g)
                chunk(("wo", m), KD, lambda k: w[:, k, (m % 2) * P:(m % 2 + 1) * P], lambda k: oT[:, k, :])
            sum_squares("n4", sq, KD, SQ["n4"])
            moe(1, 4)
            sum_squares("n5", sq, KD, SQ["n5"])
            embed(1, 5)
            sum_squares("n6", sq, KD, SQ["n6"])

        v, s = nc.vector, nc.scalar

        def vcol(name, k):
            return vt[:, VCOL[name] + k:VCOL[name] + k + 1]

        @block.vector
        def _(dve):
            steps = [0]

            def step(ins):
                steps[0] += 1
                ins.then_inc(s_dve, 1)
                dve.wait_ge(s_dve, steps[0])

            def inverse_root(key, n):
                ps = arrive(dve, key)
                v.tensor_scalar(rstd[:], ps[:, 0:T], 1.0 / n, EPS, ALU.mult, ALU.add).then_inc(is_free(key), 1)
                dve.wait_ge(s_rs, NORMS.index(key) + 1)
                step(v.reciprocal(rstd[:], rstd[:]))

            def norm(key, gain, col):
                inverse_root(key, D)
                for k in range(KD):
                    v.scalar_tensor_tensor(out=xnT[:, k, :], in0=hT[:, k, :], scalar=vcol(gain, col + k), in1=rstd[:],
                                           op0=ALU.mult, op1=ALU.mult).then_inc(s_xn, 1)

            def gained(gain, col, k):
                v.tensor_scalar(xnT[:, k, :], hT[:, k, :], vcol(gain, col + k), None, ALU.mult).then_inc(s_xn, 1)

            def add_to_h(key, k):
                ps = arrive(dve, key)
                v.tensor_tensor(hT[:, k, :], hT[:, k, :], ps[:, 0:T], ALU.add).then_inc(is_free(key), 1)

            dve.wait_ge(s_x, 16)
            dve.wait_ge(s_vec, 16)
            norm("n0", "norm_mix", 0)
            dve.wait_ge(s_dw, 16)
            dve.wait_ge(s_st, 16)
            dve.wait_ge(s_zero, 1)
            cv = 0
            tap = wdw[:].rearrange("p (j k) -> p k j", k=KD)

            def glu(c):
                key = ("pw1", 0, c)
                ps = arrive(dve, key)
                freed(dve, ("pw1", 1, c))
                v.scalar_tensor_tensor(out=uT[:, c, CW - 1:CW - 1 + TP], in0=ps[:, 0:TP], scalar=vcol("conv_b_pw1", c),
                                       in1=sgu[:, c % 4, 0:TP], op0=ALU.add, op1=ALU.mult)
                v.scalar_tensor_tensor(out=stT[:, c, :, CW - 1], in0=ps[:, TP:T], scalar=vcol("conv_b_pw1", c),
                                       in1=sgu[:, c % 4, TP:T], op0=ALU.add, op1=ALU.mult)\
                 .then_inc(is_free(key), 1)

            def sample_taps(c):
                step(v.tensor_tensor(ctmp, stT[:, c, :, :], tap[:, c, :].unsqueeze(1).to_broadcast([P, TS, CW]),
                                     ALU.mult))
                step(v.reduce_sum(zT[:, c, TP:T], ctmp, AX.X))
                v.tensor_scalar(zT[:, c, TP:T], zT[:, c, TP:T], vcol("conv_b_dw", c), None, ALU.add)\
                 .then_inc(s_z, 1)

            for c in CONV_DVE[0]:
                glu(c)
            for group in CONV_DVE:
                for c in group:
                    freed(dve, ("pw1", 0, c))
                    v.tensor_scalar(zT[:, c, 0:TP], uT[:, c, 0:TP], wdw[:, c:c + 1], vcol("conv_b_dw", c), ALU.mult,
                                    ALU.add).then_inc(s_cv, 1)
                    cv += 1
                for j in range(1, CW):
                    if group is CONV_DVE[0] and j in GLU_AT:
                        glu(len(group) + GLU_AT.index(j))
                    for c in group:
                        dve.wait_ge(s_cv, cv - len(group) + 1)
                        v.scalar_tensor_tensor(out=zT[:, c, 0:TP], in0=uT[:, c, j:j + TP],
                                               scalar=wdw[:, j * KD + c:j * KD + c + 1], in1=zT[:, c, 0:TP],
                                               op0=ALU.mult, op1=ALU.add).then_inc(s_cv, 1)
                        cv += 1
                for c in group:
                    dve.wait_ge(s_cv, cv)
                    sample_taps(c)
            dve.wait_ge(s_zp, CW)
            sample_taps(CONV_POOL)
            for c in CONV_PE:
                freed(dve, ("pw1", 0, c))
                key = ("taps", c)
                ps = arrive(dve, key)
                v.tensor_scalar(zT[:, c, 0:TP], ps[:, 0:TP], vcol("conv_b_dw", c), None, ALU.add)\
                 .then_inc(is_free(key), 1)
                sample_taps(c)
            ps = arrive(dve, "lnm")
            v.tensor_scalar(mu, ps[:, 0:T], 1.0 / D, None, ALU.mult).then_inc(is_free("lnm"), 1)
            freed(dve, "lnm")
            dve.wait_ge(s_z, KD)
            for k in range(KD):
                v.tensor_tensor(zT[:, k, :], zT[:, k, :], mu, ALU.subtract).then_inc(s_zc, 1)
            inverse_root("lnv", D)
            for k in range(KD):
                v.tensor_tensor(zT[:, k, :], zT[:, k, :], rstd[:], ALU.mult).then_inc(s_zn, 1)
            for m in range(KD):
                add_to_h(("pw2", m), m)
            for m in range(KD):
                freed(dve, ("pw2", m))
            norm("n1", "norm_ffn", 0)

            def route(l):
                L, gl8, gmx, em, G32, emx, M1, M2, M, pos, ex, eidx, gidx, gsum, den, ridx, w1, w2, slot1, slot2 = (
                    rt[n] for n in ("L", "gl8", "gmx", "em", "G32", "emx", "M1", "M2", "M", "pos", "ex", "eidx", "gidx",
                                    "gsum", "den", "ridx", "w1", "w2", "slot1", "slot2"))
                iota = cst[:, C_IOTA:C_IOTA + NPAIR]
                n3 = G + E
                key = ("router", l)
                ps = arrive(dve, key)
                dve.wait_ge(s_wr, 32)
                dve.wait_ge(s_zero, 4)
                step(v.tensor_tensor(L[:, 0:2, :], ps[:, 0:2 * n3].rearrange("p (i e) -> p i e", i=2),
                                     br[:, l, :].unsqueeze(1).to_broadcast([P, 2, n3]), ALU.add))
                v.tensor_tensor(L[0:TS, 2, :], ps[0:TS, 2 * n3:3 * n3], br[0:TS, l, :], ALU.add)\
                 .then_inc(is_free(key), 1)
                freed(dve, key)
                step(v.tensor_copy(gl8[:, :, 0:G], L[:, :, 0:G]))
                for i in range(3):
                    last = v.max(gmx[:, i, :], gl8[:, i, :])
                step(last)
                for i in range(3):
                    last = v.max_index(gix[:, i, :], gmx[:, i, :], gl8[:, i, :])
                step(last)
                step(v.tensor_copy(gidx[:], gix[:, :, 0:1]))
                step(v.tensor_tensor(G32[:], cst[:, C_GRP:C_GRP + E].unsqueeze(1).to_broadcast([P, 3, E]),
                                     gidx[:].to_broadcast([P, 3, E]), ALU.is_equal))
                step(v.tensor_tensor(em[:], L[:, :, G:n3], G32[:], ALU.mult))
                step(v.tensor_scalar(pos[:], G32[:], BIG, -BIG, ALU.mult, ALU.add))
                step(v.tensor_tensor(em[:], em[:], pos[:], ALU.add))
                for i in range(3):
                    last = v.max(emx[:, i, :], em[:, i, :])
                step(last)
                for i in range(3):
                    last = v.max_index(eix[:, i, :], emx[:, i, :], em[:, i, :])
                step(last)
                step(v.tensor_copy(eidx[:], eix[:, :, 0:2]))
                io = cst[:, C_IOTA:C_IOTA + E].unsqueeze(1).to_broadcast([P, 3, E])
                v.tensor_tensor(M1[:], io, eidx[:, :, 0:1].to_broadcast([P, 3, E]), ALU.is_equal)
                step(v.tensor_tensor(M2[:], io, eidx[:, :, 1:2].to_broadcast([P, 3, E]), ALU.is_equal))
                v.tensor_tensor(M[:], M1[:], M2[:], ALU.add).then_inc(s_hot, 1)
                v.tensor_tensor(ex[:, :, 0:G], gl8[:, :, 0:G], gmx[:, :, 0:1].to_broadcast([P, 3, G]), ALU.subtract)
                v.tensor_tensor(ex[:, :, G:G + 1], emx[:, :, 1:2], emx[:, :, 0:1], ALU.subtract).then_inc(s_pre, 1)
                key = ("rank", l)
                ps = arrive(dve, key)
                step(v.tensor_copy(cnt[:], ps[:, 3 * E:4 * E]))
                step(v.tensor_tensor_scan(incl[:], ones[:, 0:E], cnt[:], 0.0, ALU.mult, ALU.add))
                step(v.tensor_tensor(off[:], incl[:], cnt[:], ALU.subtract))
                step(v.tensor_tensor(pos[:, 0:2, :], ps[:, 0:2 * E].rearrange("p (i e) -> p i e", i=2),
                                     off[:].unsqueeze(1).to_broadcast([P, 2, E]), ALU.add))
                v.tensor_tensor(pos[0:TS, 2, :], ps[0:TS, 2 * E:3 * E], off[0:TS, :], ALU.add)\
                 .then_inc(is_free(key), 1)
                freed(dve, key)
                step(v.tensor_tensor(em[:], M1[:], pos[:], ALU.mult))
                step(v.reduce_sum(slot1[:], em[:], AX.X))
                step(v.tensor_tensor(em[:], M2[:], pos[:], ALU.mult))
                v.reduce_sum(slot2[:], em[:], AX.X).then_inc(s_slot, 1)
                dve.wait_ge(s_slot, l + 1)
                for i, (t0, n) in enumerate(TILES):
                    step(v.tensor_scalar(S[0:n, i, :], iota[0:n, :], slot1[0:n, i, :], None, ALU.is_equal))
                    v.scalar_tensor_tensor(out=S[0:n, i, :], in0=iota[0:n, :], scalar=slot2[0:n, i, :],
                                           in1=S[0:n, i, :], op0=ALU.is_equal, op1=ALU.add).then_inc(s_S, 1)
                dve.wait_ge(s_ex, l + 1)
                step(v.reduce_sum(gsum[:], ex[:, :, 0:G], AX.X))
                step(v.tensor_scalar(den[:], ex[:, :, G:G + 1], 1.0, None, ALU.add))
                step(v.tensor_tensor(den[:], den[:], gsum[:], ALU.mult))
                step(v.reciprocal(w1[:], den[:]))
                v.tensor_tensor(w2[:], w1[:], ex[:, :, G:G + 1], ALU.mult).then_inc(s_w, 1)
                step(v.tensor_copy(offI[:], off[:]))
                step(v.reduce_max(most[:], cnt[:], AX.X))
                step(v.tensor_copy(mostI[:], most[:]))
                w64 = cst[:, C_W64:C_W64 + NXW * E].rearrange("p (w e) -> p w e", w=NXW)

                def wide(x):
                    return x[:].unsqueeze(1).to_broadcast([P, NXW, E])
                step(v.tensor_tensor(xst[:], wide(off), w64, ALU.add))
                step(v.tensor_scalar(xst[:], xst[:], float(NPAIR), None, ALU.min))
                v.tensor_copy(xstI[:], xst[:]).then_inc(s_off, 1)
                for x in range(2):
                    step(v.tensor_tensor(incl[:], cst[:, C_BASE + x * E:C_BASE + (x + 1) * E], off[:], ALU.subtract))
                    base = incl[:].unsqueeze(1).to_broadcast([P, 3, E])
                    for i, (m, at) in enumerate(((M1, slot1), (M2, slot2))):
                        step(v.tensor_tensor(em[:], m[:], base, ALU.mult))
                        step(v.reduce_sum(gsum[:], em[:], AX.X))
                        step(v.tensor_tensor(ridx[:, :, i:i + 1], gsum[:], at[:], ALU.add))
                    if x == 0:
                        step(v.tensor_scalar(ridx[:], ridx[:], float(E * W - 1), None, ALU.min))
                    v.tensor_copy(idx[x][:], ridx[:]).then_inc(s_idx, 1)
                    dve.wait_ge(s_idx, 2 * l + x + 1)

            def moe(l):
                route(l)
                for hf in range(2):
                    for k in range(1, KD, 2):
                        key = ("xg", l, hf, k)
                        ps = arrive(dve, key)
                        v.tensor_copy(XGT[:, k, hf * HALF:(hf + 1) * HALF], ps[:, 0:HALF]).then_inc(is_free(key), 1)
                for hf in range(2):
                    for k in range(KD):
                        freed(dve, ("xg", l, hf, k))
                dve.wait_ge(s_pad, l + 1)
                dve.wait_ge(s_off, l + 1)
                eb = E * l

                def window_in(it, j):
                    e = 3 * it + j
                    at = dve.value_load(offI[0:1, bass.ds(e, 1)], min_val=0, max_val=NPAIR)
                    if not isinstance(e, int) or e >= 3:
                        dve.wait_ge(s_gu, e + (eb - 2))
                    v.tensor_copy(xe[:, j % 3, :, :], XGT[:, :, bass.ds(at, W)]).then_inc(s_xe, 1)

                def body(it, j):
                    e = 3 * it + j
                    if not isinstance(e, int) or e + 2 < E:
                        window_in(it, j + 2)
                    dve.wait_ge(s_sg, e + (eb + 1))
                    if not isinstance(e, int) or e >= 3:
                        dve.wait_ge(s_tr, e + (eb - 2))
                    v.tensor_tensor(hid[:, j, :], sg[:, j, :], bank[j][:, P:2 * P], ALU.mult)\
                     .then_inc(s_hid, 1)
                    dve.wait_ge(s_tr, e + (eb + 1))
                    if not isinstance(e, int) or e >= 3:
                        dve.wait_ge(s_dn, e + (eb - 2))
                    v.tensor_copy(hidT[:, j, :], bank[3][:, 0:P])\
                     .then_inc(s_ht, 1)

                window_in(0, 0)
                window_in(0, 1)
                experts(dve, body)
                for m in range(KD):
                    key = ("pin", l, m)
                    ps = arrive(dve, key)
                    v.tensor_copy(pinT[:, m, :], ps[:, 0:T]).then_inc(is_free(key), 1)
                with dve.If(dve.value_load(mostI[0:1, 0:1], min_val=0, max_val=NPAIR) > W):
                    dve.wait_ge(s_dn, eb + E)
                    with dve.Fori(0, E) as e:
                        for i in range(NXW):
                            at = dve.value_load(xstI[0:1, i, bass.ds(e, 1)], min_val=0, max_val=NPAIR)
                            v.tensor_copy(xe[:, 0, :, :], XGT[:, :, bass.ds(at, W)]).then_inc(x_xe[l], 1)
                            dve.wait_ge(x_sg[l], NXW * e + (i + 1))
                            v.tensor_tensor(hid[:, 0, :], sg[:, 0, :], bank[0][:, P:2 * P], ALU.mult)\
                             .then_inc(x_hid[l], 1)
                            dve.wait_ge(x_tr[l], NXW * e + (i + 1))
                            v.tensor_copy(hidT[:, 0, :], bank[3][:, 0:P])\
                             .then_inc(x_ht[l], 1)
                for i, (t0, n) in enumerate(TILES):
                    dve.wait_ge(s_gat[i], 32 * (l + 1))
                    dve.wait_ge(s_g1, 3 * l + i + 1)
                    v.scalar_tensor_tensor(out=R[0:n, i, 0, :], in0=R[0:n, i, 1, :], scalar=rt["w2"][0:n, i, :],
                                           in1=R[0:n, i, 0, :], op0=ALU.mult, op1=ALU.add).then_inc(s_mix, 1)
                for k in range(KD + 1):
                    if k < KD:
                        add_to_h(("mo", l, k), k)
                    if k:
                        freed(dve, ("mo", l, k - 1))
                        gained("ple_g", KD * l, k - 1)

            def embed(l):
                for m in range(KD + 1):
                    if m < KD:
                        key = ("pg", l, m)
                        ps = arrive(dve, key)
                        v.tensor_tensor(sgp[:, m % 2, :], ps[:, 0:T], rstd[:], ALU.mult).then_inc(is_free(key), 1)
                    if m:
                        dve.wait_ge(s_gb, KD * l + m)
                        step(v.tensor_tensor(tgp[:, (m - 1) % 2, :], sgp[:, (m - 1) % 2, :], pinT[:, m - 1, :],
                                             ALU.mult))
                        v.tensor_tensor(hT[:, m - 1, :], hT[:, m - 1, :], tgp[:, (m - 1) % 2, :], ALU.add)\
                         .then_inc(s_ple, 1)
                dve.wait_ge(s_ple, KD * (l + 1))

            dve.wait_ge(s_done, 32)
            moe(0)
            inverse_root("n2", D)
            embed(0)
            for k in range(KD):
                gained("norm_mix", KD, k)
            inverse_root("n3", D)
            for m in range(KQ):
                ps = arrive(dve, ("cq", m))
                v.tensor_tensor(cqr[:, m, :], ps[:, 0:T], rstd[:], ALU.mult).then_inc(is_free(("cq", m)), 1)
            for m in range(KK):
                ps = arrive(dve, ("kv", m))
                v.tensor_tensor(kvr[:, m, :], ps[:, 0:T], rstd[:], ALU.mult).then_inc(is_free(("kv", m)), 1)
            ps = arrive(dve, "kpe")
            v.tensor_tensor(kr, ps[:, 0:T], rstd[:], ALU.mult).then_inc(is_free("kpe"), 1)
            freed(dve, "kpe")
            for m in range(KQ):
                freed(dve, ("cq", m))
            for m in range(KK):
                freed(dve, ("kv", m))
            inverse_root("q", QL)
            for k in range(KQ):
                v.scalar_tensor_tensor(out=cqT[:, k, :], in0=cqr[:, k, :], scalar=vcol("mla_g_q", k), in1=rstd[:],
                                       op0=ALU.mult, op1=ALU.mult).then_inc(s_cq, 1)
            dve.wait_ge(s_cq, KQ)
            inverse_root("kv", KL)
            for k in range(KK):
                v.scalar_tensor_tensor(out=ckvT[:, k, :], in0=kvr[:, k, :], scalar=vcol("mla_g_kv", k), in1=rstd[:],
                                       op0=ALU.mult, op1=ALU.mult).then_inc(s_ck, 1)
            cos, sin = cst[:, C_COS:C_COS + T], cst[:, C_SIN:C_SIN + T]

            def rotate(key, raw, out, done):
                ps = arrive(dve, key)
                step(v.tensor_tensor(rtmp[:, 0, :], raw, cos, ALU.mult))
                v.tensor_tensor(rtmp[:, 1, :], ps[:, 0:T], sin, ALU.mult).then_inc(is_free(key), 1)
                freed(dve, key)
                v.tensor_tensor(out, rtmp[:, 0, :], rtmp[:, 1, :], ALU.add).then_inc(done, 1)

            freed(dve, "kpe")
            rotate("krot", kr, kpeT, s_kpe)
            dve.wait_ge(s_kpe, 1)
            for c in range(4):
                freed(dve, ("qp", c))
                rotate(("qrot", c), qpr[:, c, :], qpeT[:, c, :], s_qp)
                dve.wait_ge(s_qp, c + 1)
            for c in range(KD):
                ps = arrive(dve, ("kn", c))
                v.tensor_copy(knT[:, c, :], ps[:, 0:TP]).then_inc(is_free(("kn", c)), 1)
            dve.wait_ge(s_qz, 2)
            for i in range(SB):
                for g in range(4):
                    v.tensor_copy(qps[i * DR:(i + 1) * DR, i:TS:SB, g:H:4],
                                  qpeT[g * DR:(g + 1) * DR, :, TP + i:T:SB].rearrange("p c b -> p b c"))\
                     .then_inc(s_qps, 1)
            for odd in range(2):
                key = ("ql", odd)
                ps = arrive(dve, key)
                v.tensor_copy(qlat[:, :, :, odd:H:2].rearrange("p k b c -> p k c b"),
                              ps[:, 0:KK * KD * TS].rearrange("p (k c b) -> p k c b", k=KK, c=KD))\
                 .then_inc(is_free(key), 1)

            nmx = stat[:, 0:2 * H]
            esum = stat[:, 2 * H:4 * H]
            rinv = stat[:, 4 * H:6 * H]

            def head_max(h):
                key = ("sc", h)
                ps = arrive(dve, key)
                if h >= 2:
                    dve.wait_ge(s_pe, h - 1)
                v.scalar_tensor_tensor(out=sS[:, h % 2, :], in0=ps[:, 0:384], scalar=SCALE,
                                       in1=cst[:, C_MASK:C_MASK + 384], op0=ALU.mult, op1=ALU.add)\
                 .then_inc(is_free(key), 1)
                freed(dve, key)
                v.tensor_reduce(nmx[:, 2 * h:2 * h + 1], sS[:, h % 2, 0:P], AX.X, ALU.max, negate=True)
                v.tensor_reduce(nmx[:, 2 * h + 1:2 * h + 2], sS[:, h % 2, P:384], AX.X, ALU.max, negate=True)\
                 .then_inc(s_ng, 1)

            def head_norm(h):
                dve.wait_ge(s_pe, h + 1)
                step(v.reciprocal(rinv[:, 2 * h:2 * h + 2], esum[:, 2 * h:2 * h + 2]))
                v.tensor_scalar(pr[:, h % 3, 0:P], pr[:, h % 3, 0:P], rinv[:, 2 * h:2 * h + 1], None, ALU.mult)
                v.tensor_scalar(pr[:, h % 3, P:384], pr[:, h % 3, P:384], rinv[:, 2 * h + 1:2 * h + 2], None,
                                ALU.mult).then_inc(s_pn, 1)

            def head_out(c):
                ps = arrive(dve, ("o", c))
                v.tensor_copy(oT[:, c, 0:TP], ps[:, 0:TP]).then_inc(is_free(("o", c)), 1)

            def sample_max(B):
                for q2 in range(3):
                    n = 512 if q2 < 2 else 1
                    ps = arrive(dve, ("ss", B, q2))
                    if B:
                        dve.wait_ge(t_pe, B)
                    t = v.tensor_reduce(sstat[:, B, q2:q2 + 1], ps[:, 0:n], AX.X, ALU.max, negate=True)
                step(t)
                step(v.tensor_reduce(sstat[:, B, 3:4], sstat[:, B, 0:3], AX.X, ALU.min))
                v.tensor_scalar(sstat[:, B, 3:4], sstat[:, B, 3:4], SCALE, None, ALU.mult).then_inc(t_ng, 1)

            def sample_new(B):
                dve.wait_ge(t_pe, B + 1)
                v.tensor_scalar(pnew, cst[:, C_NEW:C_NEW + TS], pp[:, PAST:PAST + 1], None, ALU.mult)\
                 .then_inc(t_pn, 1)
                step(v.reduce_sum(sstat[:, B, 7:8], sstat[:, B, 4:7], AX.X))
                step(v.reciprocal(sstat[:, B, 7:8], sstat[:, B, 7:8]))

            def sample_turned(B):
                for hf in range(2):
                    key = ("sp", B, hf)
                    ps = arrive(dve, key)
                    v.tensor_copy(PTs[:, 4 * hf:4 * hf + 4, :], ps[:, :].rearrange("p (g h) -> p g h", g=4))\
                     .then_inc(is_free(key), 1)
                key = ("sn", B)
                ps = arrive(dve, key)
                v.tensor_scalar(PTn, ps[0:TS, 0:P], cst[0:TS, C_BAT + B:C_BAT + B + 1], None, ALU.mult)\
                 .then_inc(is_free(key), 1)

            def sample_rows(B):
                ps = arrive(dve, ("sv", B))
                if B:
                    arrive(dve, ("st", B - 1))
                v.tensor_scalar(orows, ps[:, 0:KL], sstat[:, B, 7:8], None, ALU.mult).then_inc(t_or, 1)
                dve.wait_ge(t_or, B + 1)
                t = v.tensor_copy(sstat[:, B, 0:1], sstat[:, B, 7:8])
                t.then_inc(is_free(("sv", B)), 1)

            def sample_latent(B):
                ps = arrive(dve, ("st", B))
                src = ps[:, 0:KK * P].rearrange("p (k i h) -> p k h i", k=KK, i=SB)
                for k in range(KK):
                    t = v.tensor_copy(olat[:, k, :, SB * B:SB * (B + 1)], src[:, k, 0:H, :])
                t.then_inc(is_free(("st", B)), 1)

            for i in range(H + 2):
                if i < H:
                    head_max(i)
                if 1 <= i <= H:
                    head_norm(i - 1)
                if i >= 5 and i % 2 == 1:
                    head_out((i - 5) // 2)
                if i == SAMPLE_AT[1]:
                    sample_new(0)
                if i - 1 in SAMPLE_AT:
                    (sample_max, sample_turned, sample_rows, sample_latent)[SAMPLE_AT.index(i - 1)](0)
            for c in range(KD):
                if (H + 1 - 5) // 2 < c:
                    head_out(c)
            sample_max(1)
            sample_new(1)
            sample_turned(1)
            sample_rows(1)
            sample_latent(1)
            ps = arrive(dve, "so")
            v.tensor_copy(oT[:, :, TP:T], ps[:, 0:KD * TS].rearrange("p (c b) -> p c b", c=KD))\
             .then_inc(is_free("so"), 1)
            for m in range(KD):
                add_to_h(("wo", m), m)
            for m in range(KD):
                freed(dve, ("wo", m))
            norm("n4", "norm_ffn", KD)
            dve.wait_ge(s_done, 32 + 64)
            moe(1)
            inverse_root("n5", D)
            embed(1)
            norm("n6", "norm_final", 0)

        @block.scalar
        def _(act):
            act.dma_start(hT[:], a["xT"]).then_inc(s_x, 16)
            act.dma_start(cst[:], a["constants"]).then_inc(s_cst, 16)
            act.dma_start(vt[:], a["vectors"]).then_inc(s_vec, 16)
            act.dma_start(wdw[:], a["tapsT"]).then_inc(s_dw, 16)
            act.dma_start(stT[:, :, :, 0:CW - 1], a["stateT"]).then_inc(s_st, 16)
            act.dma_start(pT[:], a["pT"]).then_inc(s_p, 16)
            act.dma_start(wr[:], a["w_router"]).then_inc(s_wr, 16)
            act.dma_start(br[:], a["b_router"]).then_inc(s_wr, 16)

            def squares(name, src, n, ready, at=0):
                for k in range(n):
                    ready(k)
                    s.activation(sq[:, at + k, :], src[:, k, :], ACT.Square).then_inc(s_sq, 1)

            def root(key):
                freed(act, key)
                s.activation(rstd[:], rstd[:], ACT.Sqrt).then_inc(s_rs, 1)

            def h_ready(key):
                return lambda k: freed(act, key + (k,))

            squares("n0", hT, KD, lambda k: act.wait_ge(s_x, 16))
            root("n0")
            act.wait_ge(s_vec, 16)
            for c in range(KD):
                key = ("pw1", 1, c)
                ps = arrive(act, key)
                if c >= 4:
                    freed(act, ("pw1", 0, c - 4))
                s.activation(sgu[:, c % 4, :], ps[:, 0:T], ACT.Sigmoid, bias=vcol("conv_b_pw1", KD + c))\
                 .then_inc(is_free(key), 1)
            squares("ln", zT, KD, lambda k: act.wait_ge(s_zc, k + 1))
            root("lnv")
            for k in range(KD):
                act.wait_ge(s_zn, k + 1)
                s.activation(xnT[:, k, :], zT[:, k, :], ACT.Silu, bias=vcol("conv_ln_b", k),
                             scale=vcol("conv_ln_g", k)).then_inc(s_zs, 1)
            squares("n1", hT, KD, h_ready(("pw2",)))
            root("n1")

            def moe(l):
                ex = rt["ex"]
                for i, (t0, n) in enumerate(TILES):
                    for hf in range(2):
                        key = ("row", l, i, hf)
                        ps = arrive(act, key)
                        s.copy(XR[0:n, i, hf * 512:(hf + 1) * 512], ps[0:n, :]).then_inc(is_free(key), 1)
                act.wait_ge(s_pre, l + 1)
                s.activation(ex[:], ex[:], ACT.Exp).then_inc(s_ex, 1)
                for hf in range(2):
                    for k in range(0, KD, 2):
                        key = ("xg", l, hf, k)
                        ps = arrive(act, key)
                        s.copy(XGT[:, k, hf * HALF:(hf + 1) * HALF], ps[:, 0:HALF]).then_inc(is_free(key), 1)
                act.wait_ge(s_off, l + 1)
                eb = E * l

                def window_out(it, j):
                    e = 3 * it + j
                    act.wait_ge(s_dn, e + (eb + 1))
                    if not isinstance(e, int) or e >= 3:
                        act.wait_ge(s_row[j], 32 * it + stored(l, j))
                    s.copy(orow[:, j, :], bank[4 + j][:, :]).then_inc(s_out, 1)
                    act.wait_ge(s_out, e + (eb + 1))
                    for c in range(2):
                        act.dma_start(erow[bass.ds(e, 1), :, c].rearrange("o w d -> (o w) d"),
                                      orow[64 * c:64 * c + W, j, :]).then_inc(s_row[j], 16)

                def body(it, j):
                    e = 3 * it + j
                    act.wait_ge(s_gu, e + (eb + 1))
                    if not isinstance(e, int) or e >= 3:
                        act.wait_ge(s_hid, e + (eb - 2))
                    s.activation(sg[:, j, :], bank[j][:, 0:P], ACT.Silu).then_inc(s_sg, 1)
                    if j == 0:
                        if not isinstance(it, int) or it:
                            window_out(it - 1, 2)
                    else:
                        window_out(it, j - 1)

                experts(act, body)
                window_out(E // 3, E % 3 - 1)
                with act.If(act.value_load(mostI[0:1, 0:1], min_val=0, max_val=NPAIR) > W):
                    act.wait_ge(s_hid, eb + E)
                    for j in range(3):
                        act.wait_ge(s_row[j], stored(l + 1, j))
                    with act.Fori(0, E) as e:
                        for i in range(NXW):
                            act.wait_ge(x_gu[l], NXW * e + (i + 1))
                            s.activation(sg[:, 0, :], bank[0][:, 0:P], ACT.Silu).then_inc(x_sg[l], 1)
                            act.wait_ge(x_dn[l], NXW * e + (i + 1))
                            s.copy(orow[:, 0, :], bank[4][:, :]).then_inc(x_out[l], 1)
                            act.wait_ge(x_out[l], NXW * e + (i + 1))
                            for c in range(2):
                                act.dma_start(xrow[bass.ds(e, 1), i + 1, :, c].rearrange("o w d -> (o w) d"),
                                              orow[64 * c:64 * c + W, 0, :]).then_inc(x_row[l], 16)
                            act.wait_ge(x_row[l], 32 * NXW * e + 32 * (i + 1))
                for i, (t0, n) in enumerate(TILES):
                    act.wait_ge(s_gat[i], 32 * (l + 1))
                    s.mul(R[0:n, i, 0, :], R[0:n, i, 0, :], rt["w1"][0:n, i, :]).then_inc(s_g1, 1)
                squares("n2" if l == 0 else "n5", hT, KD, h_ready(("mo", l)))
                root("n2" if l == 0 else "n5")

            def embed(l):
                for m in range(KD):
                    freed(act, ("pg", l, m))
                    s.activation(sgp[:, m % 2, :], sgp[:, m % 2, :], ACT.Sigmoid).then_inc(s_gb, 1)

            act.wait_ge(s_done, 32)
            moe(0)
            embed(0)
            squares("n3", hT, KD, lambda k: act.wait_ge(s_ple, k + 1))
            root("n3")
            squares("q", cqr, KQ, lambda k: freed(act, ("cq", k)))
            squares("kv", kvr, KK, lambda k: freed(act, ("kv", k)), at=KQ)
            root("q")
            root("kv")
            for c in range(4):
                ps = arrive(act, ("qp", c))
                s.copy(qpr[:, c, :], ps[:, 0:T]).then_inc(is_free(("qp", c)), 1)
            for m in range(KD):
                ps = arrive(act, ("qn", m))
                s.copy(qnT[:, m, :], ps[:, 0:T]).then_inc(is_free(("qn", m)), 1)
            for i in range(2):
                for hf in range(2):
                    ps = arrive(act, ("V", i, hf))
                    s.copy(V[:, i, hf * 512:(hf + 1) * 512], ps[:, :]).then_inc(is_free(("V", i, hf)), 1)
            ps = arrive(act, "ckr")
            s.copy(ckR[0:TS, :], ps[0:TS, 0:KL]).then_inc(is_free("ckr"), 1)

            nmx = stat[:, 0:2 * H]
            esum = stat[:, 2 * H:4 * H]

            def head_exp(h):
                act.wait_ge(s_ng, h + 1)
                if h >= 3:
                    arrive(act, ("pt", h - 3))
                s.activation(pr[:, h % 3, 0:P], sS[:, h % 2, 0:P], ACT.Exp, bias=nmx[:, 2 * h:2 * h + 1],
                             accum_out=esum[:, 2 * h:2 * h + 1])
                s.activation(pr[:, h % 3, P:384], sS[:, h % 2, P:384], ACT.Exp, bias=nmx[:, 2 * h + 1:2 * h + 2],
                             accum_out=esum[:, 2 * h + 1:2 * h + 2]).then_inc(s_pe, 1)

            def head_weights(h):
                ps = arrive(act, ("pt", h))
                if h >= 3:
                    arrive(act, ("o", (h - 3) // 2))
                s.copy(PT[:, h % 3, :], ps[:, 0:384]).then_inc(is_free(("pt", h)), 1)

            def sample_exp(B):
                act.wait_ge(t_ng, B + 1)
                if B:
                    arrive(act, ("sp", B - 1, 1))
                    arrive(act, ("sn", B - 1))
                for q2 in range(3):
                    n = 512 if q2 < 2 else 1
                    ps = bank[taken[("ss", B, q2)][0]]
                    s.activation(pp[:, 512 * q2:512 * q2 + n], ps[:, 0:n], ACT.Exp, bias=sstat[:, B, 3:4], scale=SCALE,
                                 accum_out=sstat[:, B, 4 + q2:5 + q2]).then_inc(is_free(("ss", B, q2)), 1)
                for q2 in range(3):
                    freed(act, ("ss", B, q2))
                s.copy(spent[:, B:B + 1], sstat[:, B, 4:5]).then_inc(t_pe, 1)

            for i in range(H + 2):
                if i < H:
                    head_exp(i)
                if i >= 2:
                    head_weights(i - 2)
                if i == SAMPLE_AT[0] + 1:
                    sample_exp(0)
            sample_exp(1)
            squares("n4", hT, KD, h_ready(("wo",)))
            root("n4")
            act.wait_ge(s_done, 32 + 64)
            moe(1)
            embed(1)
            squares("n6", hT, KD, lambda k: act.wait_ge(s_ple, KD + k + 1))
            root("n6")

        def expert_weights(l, e, c):
            w = a[("moe_w_gate", "moe_w_up", "moe_w_down")[c]][l][bass.ds(e, 1)]
            if c < 2:
                return w.rearrange("o (p k) f -> p (o k f)", k=KD)
            return w.rearrange("o (k p) f -> p (o k) f", k=FK)

        @block.gpsimd
        def _(pool):
            g = nc.gpsimd
            pool.dma_start(pages[:], a["page_table"]).then_inc(s_pg, 16)
            g.memset(uT[:, :, 0:CW - 1], 0.0).then_inc(s_zero, 1)
            g.memset(rt["L"][:], 0.0).then_inc(s_zero, 1)
            g.memset(rt["pos"][:], 0.0).then_inc(s_zero, 1)
            g.memset(rt["gl8"][:], -BIG).then_inc(s_zero, 1)

            pool.wait_ge(s_cst, 16)
            pool.wait_ge(s_dw, 16)
            for i, c in enumerate(CONV_PE):
                for j in range(CW):
                    g.tensor_scalar(dg[:, i, j, :], ident, wdw[:, j * KD + c:j * KD + c + 1], None, ALU.mult)\
                     .then_inc(s_dg, 1)

            c = CONV_POOL
            freed(pool, ("pw1", 0, c))
            g.tensor_scalar(zT[:, c, 0:TP], uT[:, c, 0:TP], wdw[:, c:c + 1], vcol("conv_b_dw", c), ALU.mult, ALU.add)\
             .then_inc(s_zp, 1)
            for j in range(1, CW + 1):
                if j < CW:
                    if j >= 3:
                        pool.wait_ge(s_zp, j - 1)
                    g.tensor_scalar(tapped[:, j % 2, :], uT[:, c, j:j + TP], wdw[:, j * KD + c:j * KD + c + 1], None,
                                    ALU.mult).then_inc(s_zm, 1)
                if j > 1:
                    pool.wait_ge(s_zm, j - 1)
                    pool.wait_ge(s_zp, j - 1)
                    g.tensor_tensor(zT[:, c, 0:TP], zT[:, c, 0:TP], tapped[:, (j - 1) % 2, :], ALU.add)\
                     .then_inc(s_zp, 1)

            freed(pool, ("pw1", 0, KD - 1))
            pool.dma_start(out["csp"], uT[:, :, TP:TP + CW - 1]).then_inc(s_done, 16)
            pool.dma_start(out["css"], stT[:, :, :, 1:CW]).then_inc(s_done, 16)
            made = [0]

            def step(ins):
                made[0] += 1
                ins.then_inc(s_pl, 1)
                pool.wait_ge(s_pl, made[0])

            def moe(l):
                arrive(pool, ("router", l))
                pool.wait_ge(s_done, 32 + 64 * l)
                g.memset(XGT[:, :, NPAIR:XCOLS], 0.0).then_inc(s_pad, 1)
                def gather(rows, at):
                    for i, (t0, n) in enumerate(TILES):
                        for c in range(2):
                            g.indirect_dma_start(R[0:n, i, c, :], None, rows,
                                                 bass.IndirectOffsetOnAxis(at[0:n, i, c:c + 1], 0))\
                             .then_inc(s_gat[i], 16)

                pool.wait_ge(s_off, l + 1)
                arrive(pool, ("xg", l, 1, KD - 1))
                most_pairs = pool.value_load(mostI[0:1, 0:1], min_val=0, max_val=NPAIR)
                with pool.If(most_pairs > W):
                    with pool.Fori(0, E) as e:
                        for c in range(3):
                            pool.dma_start(exw[:, c, :] if c < 2 else exw[:, c, :].rearrange("p (k f) -> p k f", k=FK),
                                           expert_weights(l, e, c)).then_inc(x_w[l], 16)
                        pool.wait_ge(x_dn[l], NXW * e + NXW)
                    for j in range(3):
                        pool.wait_ge(s_row[j], stored(l + 1, j))
                    pool.dma_start(xrow[:, 0], erow).then_inc(x_copy[l], 16)
                    pool.wait_ge(x_copy[l], 16)
                    pool.wait_ge(x_row[l], 32 * NXW * E)
                    pool.wait_ge(s_idx, 2 * l + 2)
                    gather(xrows, idx[1])
                with pool.If(most_pairs <= W):
                    pool.wait_ge(s_idx, 2 * l + 2)
                    for j in range(3):
                        pool.wait_ge(s_row[j], stored(l + 1, j))
                    gather(erows, idx[0])

            def load_kpe(B):
                for i in range(SB):
                    with pool.Fori(0, PAGES) as n:
                        pg = pool.value_load(pages[0:1, bass.ds(n + (SB * B + i) * PAGES, 1)], min_val=0,
                                             max_val=NPOOL - 1)
                        pool.dma_start(KPT[DR * i:DR * (i + 1), bass.ds(n * PAGE, PAGE)],
                                       a["cache_kpeT"][bass.ds(pg, 1)].rearrange("o p f -> p (o f)"))\
                            .then_inc(s_kpin, 16)

            moe(0)
            arrive(pool, ("mo", 0, KD - 1))
            pool.wait_ge(s_pg, 16)
            pool.dma_start(wukT, a["ukT"]).then_inc(s_uk, 16)
            arrive(pool, "kpe")
            g.memset(qlat, 0.0).then_inc(s_qz, 1)
            g.memset(qps, 0.0).then_inc(s_qz, 1)
            load_kpe(0)
            pool.wait_ge(s_ck, KK)
            pool.dma_start(out["ckv_p"], ckvT[:, :, 0:TP]).then_inc(s_done, 16)
            pool.dma_start(out["ckv_s"], ckvT[:, :, TP:T]).then_inc(s_done, 16)
            pool.wait_ge(s_kpe, 1)
            pool.dma_start(out["kpe_p"], kpeT[0:DR, 0:TP]).then_inc(s_done, 16)
            pool.dma_start(out["kpe_s"], kpeT[0:DR, TP:T]).then_inc(s_done, 16)
            arrive(pool, ("ss", 0, 1))
            load_kpe(1)
            moe(1)

        @block.sync
        def _(sp):
            last = {}
            for c in range(KD):
                last[G_PW1 + c] = ("pw1", c % 2, 2 * (c // 2) + 1)
            for i in range(4):
                last[G_PW2 + i] = ("pw2", 2 * i + 1)
                last[G_WO + i] = ("wo", 2 * i + 1)
                for l in range(2):
                    last[G_PLE[l] + 1 + i] = ("pg", l, 2 * i + 1)
            for l in range(2):
                last[G_PLE[l]] = ("pin", l, KD - 1)
            for i in range(2):
                last[G_DQ + i] = ("cq", KQ - 1)
                last[G_DKV + i] = "kpe"
            for k in range(KQ):
                last[G_UQ + k] = ("sv", 1)
            last[G_UK] = ("sv", 1)
            last[G_UV] = "so"

            def used_up(g):
                g -= NSLOT
                if g < 0:
                    return
                if g in last:
                    b, u = taken[last[g]]
                    sp.wait_ge(full[b], u + 1)
                else:
                    l = int(g >= G_MOE1)
                    e, c = divmod(g - G_MOE[l], 3)
                    sp.wait_ge(s_gu if c < 2 else s_dn, E * l + e + 1)

            def fill(g):
                used_up(g)
                at = g - (3 * E if g > G_MOE0 else 0) - (3 * E if g > G_MOE1 else 0)
                sp.dma_start(slot(g), a["stream"][at]).then_inc(w_in[g % NSLOT], 16)

            def page_numbers(b):
                return [sp.value_load(pages[0:1, b * PAGES + n:b * PAGES + n + 1], min_val=0, max_val=NPOOL - 1)
                        for n in range(PAGES)]

            def load_cache(b, pg):
                if b >= SB:
                    arrive(sp, ("sv", b // SB - 1))
                elif b >= 2:
                    arrive(sp, (("qn", KD - 1), ("kn", KD - 1))[b - 2])
                for n in range(PAGES):
                    sp.dma_start(CKX[b % SB][:, n, :], a["cache_ckv"][bass.ds(pg[n], 1)].rearrange("o p f -> p (o f)"))\
                        .then_inc(s_ckin[b % SB], 16)

            def expert(l, it, j):
                e = 3 * it + j
                for c in range(3):
                    g = G_MOE[l] + 3 * j + c
                    if isinstance(it, int):
                        used_up(g + NSLOT * it)
                    else:
                        sp.wait_ge(s_gu if c < 2 else s_dn, e + (E * l - 2))
                    d = slot(g) if c < 2 else slot(g).rearrange("p (k f) -> p k f", k=FK)
                    sp.dma_start(d, expert_weights(l, e, c)).then_inc(w_in[g % NSLOT], 16)

            for g in range(G_MOE0):
                fill(g)
            experts(sp, lambda it, j: expert(0, it, j))
            fill(G_PLE0)
            fill(G_PLE0 + 1)
            for i in range(3):
                sp.wait_ge(s_gat[i], 32)
            for g in range(G_PLE0 + 2, G_MOE1):
                fill(g)
            sp.wait_ge(s_pg, 16)
            arrive(sp, "kpe")
            arrive(sp, "kv")
            for B in range(TS // SB):
                numbers = [page_numbers(SB * B + i) for i in range(SB)]
                for i in range(SB):
                    load_cache(SB * B + i, numbers[i])
            experts(sp, lambda it, j: expert(1, it, j))
            fill(G_PLE1)
            fill(G_PLE1 + 1)
            for i in range(3):
                sp.wait_ge(s_gat[i], 64)
            for g in range(G_PLE1 + 2, NPIECE):
                fill(g)
            sp.wait_ge(s_xn, 7 * KD)
            sp.dma_start(out["y_p"], xnT[:, :, 0:TP]).then_inc(s_y, 16)
            sp.dma_start(out["y_s"], xnT[:, :, TP:T]).then_inc(s_y, 16)
            sp.wait_ge(s_y, 32)
            sp.wait_ge(s_done, 16 * 6)


def packed(x):
    def chunks(w):
        w = w.reshape(-1, P, *w.shape[1:])
        return np.swapaxes(w, 0, 1)

    def piece(w):
        w = chunks(w).reshape(P, -1)
        return np.concatenate([w, np.zeros((P, SLOT - w.shape[1]), w.dtype)], 1)

    b = {}
    b["xT"] = chunks(np.concatenate([x["x_prompt"][0], x["x_sample"][:, 0]], 0).T)
    p = np.concatenate([x["p_prompt"][:, 0], x["p_sample"][:, :, 0]], 1)
    b["pT"] = np.swapaxes(np.stack([chunks(p[l].T) for l in range(2)]), 0, 1)
    b["vectors"] = np.concatenate([x[n].reshape(-1, P) for n, _ in VEC], 0).T
    b["tapsT"] = x["conv_w_dw"].reshape(CW * KD, P).T
    b["stateT"] = chunks(np.transpose(x["state_conv"][0], (2, 0, 1)))
    wr = np.concatenate([x["moe_w_group"], x["moe_w_expert"]], 2)
    b["w_router"] = np.swapaxes(np.stack([chunks(wr[l]) for l in range(2)]), 0, 1)
    br = np.concatenate([x["moe_b_group"], x["moe_b_expert"]], 1)
    b["b_router"] = np.broadcast_to(br[None], (P, 2, G + E))
    b["page_table"] = x["page_table"].reshape(1, -1)
    ckv = x["cache_ckv"][:, 0]
    ckvT = np.swapaxes(np.swapaxes(ckv, 1, 2).reshape(-1, KK, P, PAGE), 1, 2).reshape(-1, P, KK * PAGE)
    b["cache_ckv"] = np.concatenate([ckv, ckvT], 2)
    b["cache_kpeT"] = np.swapaxes(x["cache_kpe"][:, 0], 1, 2)
    b["ukT"] = chunks(np.transpose(x["mla_w_uk"][0], (1, 2, 0)).reshape(H * DN, KL))
    s = []
    for i in range(4):
        for kind in range(2):
            s.append(x["conv_w_pw1"][0][:, (4 * kind + i) * 256:(4 * kind + i + 1) * 256])
    s += [x["conv_w_pw2"][0][:, i * 256:(i + 1) * 256] for i in range(4)]

    def ple(l):
        return [x["ple_w_in"][l]] + [x["ple_w_gate"][l][:, i * 256:(i + 1) * 256] for i in range(4)]
    s += ple(0)
    s += [x["mla_w_dq"][0][512 * i:512 * (i + 1)] for i in range(2)]
    dkv = x["mla_w_dkv"][0]
    dkv = np.concatenate([dkv[:, 0:KL]] + [dkv[:, KL:]] * (P // DR), 1)
    s += [dkv[512 * i:512 * (i + 1)] for i in range(2)]
    uq = x["mla_w_uq"][0].reshape(QL, H, DN + DR)
    uq = np.concatenate([uq[:, :, 0:DN].reshape(QL, -1), uq[:, :, DN:].reshape(QL, -1)], 1)
    s += [uq[P * k:P * (k + 1)] for k in range(KQ)]
    s += [x["mla_w_uk"][0].reshape(KL, H * DN), x["mla_w_uv"][0].reshape(KL, H * DV)]
    s += [x["mla_w_o"][0][:, i * 256:(i + 1) * 256] for i in range(4)]
    s += ple(1)
    b["stream"] = np.stack([piece(w) for w in s])
    for n in ("moe_w_gate", "moe_w_up", "moe_w_down"):
        b[n] = x[n]
    b["constants"] = constants()
    return {n: np.ascontiguousarray(w) for n, w in b.items()}


_OUTS = {"y_p": (P, KD, TP), "y_s": (P, KD, TS), "csp": (P, KD, CW - 1), "css": (P, KD, TS, CW - 1),
         "ckv_p": (P, KK, TP), "kpe_p": (DR, TP), "ckv_s": (P, KK, TS), "kpe_s": (DR, TS)}


def kernel(**inputs):
    import concourse.bacc as bacc
    from concourse.bass_utils import run_bass_kernel_spmd as run

    nc = bacc.Bacc("TRN2", target_bir_lowering=False, num_devices=1)
    arrays = packed({n: np.asarray(x) for n, x in inputs.items()})
    a = {n: nc.dram_tensor("in_" + n, x.shape, mybir.dt.from_np(x.dtype), kind="ExternalInput").ap()
         for n, x in arrays.items()}
    out = {n: nc.dram_tensor("out_" + n, shape, F32, kind="ExternalOutput").ap() for n, shape in _OUTS.items()}
    erows = nc.dram_tensor("erows", (E * W, D), F32, kind="Internal").ap()
    xrows = nc.dram_tensor("xrows", (E * XROWS, D), F32, kind="Internal").ap()
    build(nc, a, out, erows, xrows)
    r = run(nc, [{"in_" + n: x for n, x in arrays.items()}], core_ids=[0]).results[0]

    def rows(name):
        y = np.moveaxis(r["out_" + name], 0, 1)
        return np.moveaxis(y.reshape(-1, *y.shape[2:]), 0, -1)

    return (rows("y_p")[None], rows("y_s")[:, None], rows("csp")[None, None], rows("css")[None],
            rows("ckv_p")[None, None], r["out_kpe_p"].T[None, None], rows("ckv_s")[None, :, None],
            r["out_kpe_s"].T[None, :, None])
```
